# Optimizing a Trainium2 kernel written in Bass

```python
import jax, jax.numpy as jnp
from jax import lax
import numpy as np

D_MODEL = 1024
BATCH = 1
SEQ = 1024
DEPTH = 1

N_META = 16
EPS = 1e-6
MLA_HEADS = 8
Q_LORA_RANK = 384
KV_LORA_RANK = 256
QK_NOPE_DIM = 128
QK_ROPE_DIM = 64
V_HEAD_DIM = 128
MLA_WIDTH = MLA_HEADS * V_HEAD_DIM
ROPE_THETA = 10000.0
Q_BLOCK = 128
HGRN_KEY_DIM = 128
HGRN_HEADS = D_MODEL // HGRN_KEY_DIM
HGRN_VAL_DIM = D_MODEL // HGRN_HEADS
HGRN_K_WIDTH = HGRN_HEADS * HGRN_KEY_DIM
HGRN_V_WIDTH = HGRN_HEADS * HGRN_VAL_DIM
CHUNK = 64
SUB_CHUNK = 16
N_SUB = CHUNK // SUB_CHUNK
HGRN_PAD = CHUNK - N_META
D_FF = -(-8 * D_MODEL // (3 * 256)) * 256
IN_SIZES = [Q_LORA_RANK, KV_LORA_RANK, QK_ROPE_DIM,
            HGRN_K_WIDTH, HGRN_K_WIDTH, HGRN_K_WIDTH, HGRN_V_WIDTH, HGRN_V_WIDTH,
            D_MODEL, D_MODEL]
IN_WIDTH = int(sum(IN_SIZES))
IN_SPLIT = [int(v) for v in np.cumsum(IN_SIZES)[:-1]]

kernel_name = "hybrid_mla_hgrn2_gated_encoder"

def rms_norm(x, gain):
    xf = x.astype(jnp.float32)
    y = xf * lax.rsqrt(jnp.mean(xf * xf, axis=-1, keepdims=True) + EPS)
    return (y * gain.astype(jnp.float32)).astype(x.dtype)

def rope_tables(length):
    inv = ROPE_THETA ** (-jnp.arange(0, QK_ROPE_DIM, 2, dtype=jnp.float32) / QK_ROPE_DIM)
    ang = jnp.arange(length, dtype=jnp.float32)[:, None] * inv[None, :]
    return jnp.cos(ang), jnp.sin(ang)

def apply_rope(x, cos, sin):
    xf = x.astype(jnp.float32)
    x1, x2 = jnp.split(xf, 2, axis=-1)
    return jnp.concatenate([x1 * cos - x2 * sin, x2 * cos + x1 * sin], axis=-1).astype(x.dtype)

def mla(c_q, c_kv, k_rope_raw, g_cq, g_ckv, w_uq, w_ukv, cos, sin):
    B, L, _ = c_q.shape
    q = (rms_norm(c_q, g_cq) @ w_uq).reshape(B, L, MLA_HEADS, QK_NOPE_DIM + QK_ROPE_DIM)
    q_nope, q_rope = q[..., :QK_NOPE_DIM], q[..., QK_NOPE_DIM:]
    q_rope = apply_rope(q_rope, cos[:, None, :], sin[:, None, :])
    kv = (rms_norm(c_kv, g_ckv) @ w_ukv).reshape(B, L, MLA_HEADS, QK_NOPE_DIM + V_HEAD_DIM)
    k_nope, v = kv[..., :QK_NOPE_DIM], kv[..., QK_NOPE_DIM:]
    k_rope = apply_rope(k_rope_raw, cos, sin)
    scale = (QK_NOPE_DIM + QK_ROPE_DIM) ** -0.5

    def attend(qn, qr):
        s = (jnp.einsum('bqhd,bkhd->bhqk', qn, k_nope)
             + jnp.einsum('bqhr,bkr->bhqk', qr, k_rope)).astype(jnp.float32) * scale
        p = jax.nn.softmax(s, axis=-1).astype(v.dtype)
        return jnp.einsum('bhqk,bkhd->bqhd', p, v)

    o_meta = attend(q_nope[:, :N_META], q_rope[:, :N_META])
    n_blk = (L - N_META) // Q_BLOCK

    def blocks(t):
        return jnp.moveaxis(t[:, N_META:].reshape(B, n_blk, Q_BLOCK, *t.shape[2:]), 1, 0)

    o_real = lax.map(lambda a: attend(a[0], a[1]), (blocks(q_nope), blocks(q_rope)))
    o_real = jnp.moveaxis(o_real, 0, 1).reshape(B, L - N_META, MLA_HEADS, V_HEAD_DIM)
    return jnp.concatenate([o_meta, o_real], axis=1).reshape(B, L, MLA_WIDTH)

def gla_chunkwise(q, k, v, g):
    B, H, T, dk = q.shape
    dv = v.shape[-1]
    n = T // CHUNK

    def chunks(t):
        return jnp.moveaxis(t.reshape(B, H, n, CHUNK, t.shape[-1]), 2, 0)

    valid = (jnp.arange(CHUNK)[None, :] < (jnp.arange(N_SUB)[:, None] + 1) * SUB_CHUNK)[:, :, None]
    causal = jnp.tril(jnp.ones((CHUNK, CHUNK), dtype=bool))

    def step(S, inp):
        q_c, k_c, v_c, g_c = inp
        b = jnp.cumsum(g_c, axis=2)
        bs = b.reshape(B, H, N_SUB, SUB_CHUNK, dk)
        gs = g_c.reshape(B, H, N_SUB, SUB_CHUNK, dk)
        b_ref = bs[:, :, :, 0] - gs[:, :, :, 0]
        q_r = q_c.reshape(B, H, N_SUB, SUB_CHUNK, dk) * jnp.exp(bs - b_ref[:, :, :, None])
        expo = b_ref[:, :, :, None, :] - b[:, :, None, :, :]
        k_r = jnp.where(valid, k_c[:, :, None] * jnp.exp(jnp.where(valid, expo, 0.0)), 0.0)
        a = jnp.einsum('bhitd,bhisd->bhits', q_r, k_r).reshape(B, H, CHUNK, CHUNK)
        a = jnp.where(causal, a, 0.0)
        o = jnp.einsum('bhts,bhsv->bhtv', a, v_c) + jnp.einsum('bhtd,bhdv->bhtv', q_c * jnp.exp(b), S)
        b_last = b[:, :, -1:]
        S = jnp.exp(b_last)[:, :, 0, :, None] * S + jnp.einsum(
            'bhcd,bhcv->bhdv', k_c * jnp.exp(b_last - b), v_c)
        return S, o

    S0 = jnp.zeros((B, H, dk, dv), jnp.float32)
    _, o = lax.scan(step, S0, (chunks(q), chunks(k), chunks(v), chunks(g)))
    return jnp.moveaxis(o, 0, 2).reshape(B, H, T, dv)

def hgrn2(q_raw, f_fwd, f_bwd, i_raw, g_raw, lb, g_norm):
    B, L, _ = q_raw.shape
    pad = ((0, 0), (0, 0), (HGRN_PAD, 0), (0, 0))

    def heads(t, d):
        return jnp.pad(t.reshape(B, L, HGRN_HEADS, d).transpose(0, 2, 1, 3), pad)

    q = heads(jax.nn.silu(q_raw), HGRN_KEY_DIM)
    v = heads(i_raw, HGRN_VAL_DIM)

    def direction(f_logit, lb_d, flip):
        f = lb_d + (1.0 - lb_d) * jax.nn.sigmoid(f_logit.astype(jnp.float32))
        k = heads((1.0 - f).astype(q.dtype), HGRN_KEY_DIM)
        g = heads(jnp.log(f), HGRN_KEY_DIM)
        if flip:
            rev = lambda t: jnp.flip(t, axis=2)
            return rev(gla_chunkwise(rev(q), rev(k), rev(v), rev(g)))
        return gla_chunkwise(q, k, v, g)

    o = direction(f_fwd, lb[0], False) + direction(f_bwd, lb[1], True)
    o = rms_norm(o[:, :, HGRN_PAD:], g_norm)
    o = o.transpose(0, 2, 1, 3).reshape(B, L, HGRN_V_WIDTH).astype(q_raw.dtype)
    return o * jax.nn.silu(g_raw)

def setup_inputs(seed: int = 0) -> dict:
    key = jax.random.key(seed)
    ks = jax.random.split(key, 20)
    f32 = jnp.float32
    nrm = lambda k, shape, fan_in: jax.random.normal(k, shape, f32) * fan_in ** -0.5
    gain = lambda k, shape: 1.0 + 0.02 * jax.random.normal(k, shape, f32)
    return {
        "x": jax.random.normal(ks[0], (BATCH, SEQ, D_MODEL), f32),
        "meta_tokens": jax.random.normal(ks[1], (N_META, D_MODEL), f32),
        "g_mix_pre": gain(ks[2], (DEPTH, D_MODEL)),
        "w_in": nrm(ks[3], (DEPTH, D_MODEL, IN_WIDTH), D_MODEL),
        "g_cq": gain(ks[4], (DEPTH, Q_LORA_RANK)),
        "g_ckv": gain(ks[5], (DEPTH, KV_LORA_RANK)),
        "w_uq": nrm(ks[6], (DEPTH, Q_LORA_RANK, MLA_HEADS * (QK_NOPE_DIM + QK_ROPE_DIM)), Q_LORA_RANK),
        "w_ukv": nrm(ks[7], (DEPTH, KV_LORA_RANK, MLA_HEADS * (QK_NOPE_DIM + V_HEAD_DIM)), KV_LORA_RANK),
        "lb_logits": 0.1 * jax.random.normal(ks[8], (DEPTH + 1, 2, HGRN_K_WIDTH), f32),
        "g_hgrn": gain(ks[9], (DEPTH, HGRN_VAL_DIM)),
        "w_o": nrm(ks[10], (DEPTH, D_MODEL, D_MODEL), D_MODEL),
        "g_mix_post": gain(ks[11], (DEPTH, D_MODEL)),
        "g_ffn_pre": gain(ks[12], (DEPTH, D_MODEL)),
        "w_gate": nrm(ks[13], (DEPTH, D_MODEL, D_FF), D_MODEL),
        "w_up": nrm(ks[14], (DEPTH, D_MODEL, D_FF), D_MODEL),
        "w_down": nrm(ks[15], (DEPTH, D_FF, D_MODEL), D_FF),
        "g_ffn_post": gain(ks[16], (DEPTH, D_MODEL)),
    }

def reference(x, meta_tokens, g_mix_pre, w_in, g_cq, g_ckv, w_uq, w_ukv, lb_logits, g_hgrn,
              w_o, g_mix_post, g_ffn_pre, w_gate, w_up, w_down, g_ffn_post):
    B = x.shape[0]
    meta = jnp.broadcast_to(meta_tokens.astype(x.dtype)[None], (B, N_META, D_MODEL))
    h = jnp.concatenate([meta, x], axis=1)
    L = h.shape[1]
    cos, sin = rope_tables(L)
    lb_all = jnp.cumsum(jax.nn.softmax(lb_logits.astype(jnp.float32), axis=0), axis=0)
    for l in range(DEPTH):
        hn = rms_norm(h, g_mix_pre[l])
        proj = hn @ w_in[l]
        c_q, c_kv, k_rope, hq, hf_fwd, hf_bwd, hi, hg, gate_a, gate_h = jnp.split(proj, IN_SPLIT, axis=-1)
        a = mla(c_q, c_kv, k_rope, g_cq[l], g_ckv[l], w_uq[l], w_ukv[l], cos, sin)
        r = hgrn2(hq, hf_fwd, hf_bwd, hi, hg, lb_all[l], g_hgrn[l])
        mixed = jax.nn.sigmoid(gate_a) * a + jax.nn.sigmoid(gate_h) * r
        h = h + rms_norm(mixed @ w_o[l], g_mix_post[l])
        hn = rms_norm(h, g_ffn_pre[l])
        ff = (jax.nn.silu(hn @ w_gate[l]) * (hn @ w_up[l])) @ w_down[l]
        h = h + rms_norm(ff, g_ffn_post[l])
    return h[:, N_META:]


_drawn_inputs = setup_inputs


def setup_inputs(seed=0):
    import zlib

    import numpy as np

    out = dict(_drawn_inputs(seed))
    spreads = {}
    factors = {'meta_tokens': 2.798,
     'g_cq': 8.0,
     'g_ckv': 8.0,
     'lb_logits': 22.475,
     'g_hgrn': 25.128,
     'g_mix_post': 3.428,
     'g_ffn_pre': 3.474,
     'g_ffn_post': 17.473}
    for name, (base, spread) in spreads.items():
        noise = np.random.default_rng([zlib.crc32(name.encode()), seed]).standard_normal(out[name].shape)
        drawn = base * np.exp(spread * noise) if base else spread * noise
        out[name] = __import__('jax').numpy.asarray(drawn.astype(out[name].dtype))
    for name, factor in factors.items():
        out[name] = (out[name] * factor).astype(out[name].dtype)
    return out
```

```python
from contextlib import ExitStack

import numpy as np

import concourse.bass as bass
from concourse import mybir

F32 = mybir.dt.float32
F32R = mybir.dt.float32r
U32 = mybir.dt.uint32
ACT = mybir.ActivationFunctionType
ALU = mybir.AluOpType
AX = mybir.AxisListType

P = 128
D = 1024
SEQ = 1024
META = 16
L = SEQ + META
EPS = 1e-6
KT = D // P
HEADS = 8
Q_RANK, KV_RANK, ROPE = 384, 256, 64
QT, KVT = Q_RANK // P, KV_RANK // P
SM_SCALE = (P + ROPE) ** -0.5
D_FF = 2816
FT = D_FF // P
CH = 128
NCH = SEQ // CH
SUB = 16
QUARTER = D // 4
HALF = 512
GC = HALF // CH
TT = SEQ // P
CHUNKS2 = [(0, HALF), (HALF, HALF)]
CHUNKS3 = [(0, 348), (348, 346), (694, 346)]
IN_HGRN = ["ff", "fb", "q", "hg", "gh", "ga"]


class At:

    def __init__(self, base, j=None, step=1):
        self.base, self.j, self.step = base, j, step

    def count(self, per, k, lag=0):
        n = (self.base - lag) * per + k
        return n if self.j is None else self.j * (per * self.step) + n

    def index(self):
        return self.base if self.j is None else self.j * self.step + self.base


class Signal:

    def __init__(self, sem, per):
        self.sem, self.per = sem, per

    def wait(self, eng, at, k, lag=0):
        n = at.count(self.per, k, lag)
        if at.j is None and n <= 0:
            return
        assert at.j is not None or n > 0
        eng.wait_ge(self.sem, n)


def three(pe, out, wh, wl, xh, xl, start, stop):
    pe.matmul(out, wh, xh, start=start, stop=False)
    pe.matmul(out, wh, xl, start=False, stop=False)
    return pe.matmul(out, wl, xh, start=False, stop=stop)



class Weights:

    def __init__(self, t, sb):
        self.raw, self.hi, self.lo = (sb(f"w_{n}", [P, 2 * KT * P], dt)
                                      for n, dt in (("raw", F32), ("hi", F32R), ("lo", F32R)))
        self.sem_in = [Signal(t.sem(f"w_in{i}"), 3 * 16) for i in range(2)]
        self.hi_done, self.lo_done = Signal(t.sem("w_hi_done"), 6), Signal(t.sem("w_lo_done"), 6)

    def of_part(self):
        return [x[:].rearrange("p (k m) -> p k m", k=KT) for x in (self.raw, self.hi, self.lo)]

    def of_blocks(self):
        return (*self.blocks(), self.sem_in, self.hi_done, self.lo_done)

    def blocks(self):
        return [[x[:, i * KT * P:(i + 1) * KT * P].rearrange("p (k m) -> p k m", k=KT) for i in range(2)]
                for x in (self.raw, self.hi, self.lo)]

    def halves_of_second(self):
        return [[x[:, KT * P + i * HALF:KT * P + (i + 1) * HALF] for i in range(2)]
                for x in (self.raw, self.hi, self.lo)]


def normalize_and_values(nc, t, hn_hi, hn_lo, weights):
    with ExitStack() as c:
        def sb(name, shape, dt=F32):
            return c.enter_context(nc.sbuf_tensor(name, shape, dt))

        X = sb("X", [P, KT, L])
        square = [t.raw[:, i * L:(i + 1) * L] for i in range(2)]
        square_sum, rs = t.raw[:, 2 * L:3 * L], t.raw[:, 3 * L:4 * L]
        first_slot = weights.of_part()
        vw_raw, vw_hi, vw_lo = ([first_slot[i], sb(f"vw_{n}", [P, KT, QUARTER], dt)[:]]
                                for i, (n, dt) in enumerate((("raw", F32), ("hi", F32R), ("lo", F32R))))
        block_raw, block_hi, block_lo, block_in, block_hi_done, block_lo_done = weights.of_blocks()
        stage = [sb(f"v_stage{i}", [P, QUARTER]) for i in range(2)]
        meta_hi, meta_lo = sb("meta_hi", [P, KT, P], F32R), sb("meta_lo", [P, KT, P], F32R)
        logits = sb("logits", [P, 2, 2 * HEADS])
        BANKS = 7
        bank = [c.enter_context(nc.psum_tensor(f"n_bank{i}", [P, HALF], F32)) for i in range(BANKS)]
        sem = t.sem
        consts_in, lb_in = sem("consts_in"), sem("lb_in")
        x_in = [sem(f"x_in{k}") for k in range(KT)]
        vw_in = [sem(f"vw_in{i}") for i in range(2)]
        squared, added, summed, rs_ready = sem("squared"), sem("added"), sem("summed"), sem("rs_ready")
        scaled, hi_done, padded = sem("scaled"), sem("hn_hi_done"), sem("hn_padded")
        lo_done = {"dve": sem("hn_lo_by_dve"), "pool": sem("hn_lo_by_pool")}
        lb_diff, lb_sig = sem("lb_diff"), sem("lb_sig")
        vw_hi_done, vw_lo_done = sem("vw_hi_done"), sem("vw_lo_done")
        v_done, v_copied = sem("v_done"), sem("v_copied")
        v_out = [sem(f"v_out{i}") for i in range(2)]
        units = [(part, tile) for part in range(4) for tile in range(TT + 1)]
        LO_BY_POOL = [3, 5, 7]
        LO_BY_DVE = [k for k in range(KT) if k not in LO_BY_POOL]

        def wait_lo(eng, k):
            if k in LO_BY_POOL:
                eng.wait_ge(lo_done["pool"], LO_BY_POOL.index(k) + 1)
            else:
                eng.wait_ge(lo_done["dve"], LO_BY_DVE.index(k) + 1)

        def make_lo(eng, k):
            by = "pool" if k in LO_BY_POOL else "dve"
            eng.wait_ge(scaled, k + 1)
            eng.wait_ge(hi_done, k + 1)
            eng.tensor_tensor(hn_lo[:, k, :], X[:, k, :], hn_hi[:, k, :].bitcast(F32), ALU.subtract
                              ).then_inc(lo_done[by], 1)

        with nc.Block() as block:
            @block.sync
            def _(sp):
                for k in range(KT):
                    sp.dma_start(X[:, k, :], t.d["x"][:, k, :]).then_inc(x_in[k], 16)
                sp.dma_start(t.consts[:], t.d["consts"]).then_inc(consts_in, 16)
                sp.dma_start(t.gains[:], t.d["gains"]).then_inc(consts_in, 16)
                sp.dma_start(logits[:], t.d["logits"]).then_inc(lb_in, 16)
                for part in range(4):
                    if part >= 2:
                        sp.wait_ge(vw_hi_done, part - 1)
                        sp.wait_ge(vw_lo_done, part - 1)
                    sp.dma_start(vw_raw[part % 2], t.d["vw"][part]).then_inc(vw_in[part % 2], 16)
                for n, (part, tile) in enumerate(units):
                    rows = P if tile < TT else META
                    sp.wait_ge(v_copied, n + 1)
                    sp.dma_start(t.d_v[0:rows, tile, part * QUARTER:(part + 1) * QUARTER],
                                 stage[n % 2][0:rows, :]).then_inc(v_out[n % 2], 16)
                    if (part, tile) == (2, TT):
                        sp.wait_ge(vw_hi_done, 3)
                        sp.wait_ge(vw_lo_done, 3)
                        for i in range(2):
                            sp.dma_start(block_raw[i], t.d["w_hgrn"][i]).then_inc(block_in[i].sem, 16)
                for i in range(2):
                    sp.wait_ge(v_out[i], 16 * (len(units) // 2))

            @block.scalar
            def _(act):
                act.preload_act_table_set("natural_log_exp_and_others")
                for k in range(KT):
                    act.wait_ge(x_in[k], 16)
                    if k >= 2:
                        act.wait_ge(added, max(k - 2, 1))
                    act.activation(square[k % 2], X[:, k, :], ACT.Square).then_inc(squared, 1)

                def split(part):
                    act.wait_ge(vw_in[part % 2], 16 * (part // 2 + 1))
                    if part >= 2:
                        act.wait_ge(v_done, (TT + 1) * (part - 1))
                    act.copy(vw_hi[part % 2], vw_raw[part % 2]).then_inc(vw_hi_done, 1)

                act.wait_ge(consts_in, 32)
                act.wait_ge(summed, 1)
                for i, (a, n) in enumerate(CHUNKS3):
                    act.activation(rs[:, a:a + n], bank[i][:, 0:n], ACT.Ln, bias=t.gain("eps", 0),
                                   scale=1.0 / D).then_inc(rs_ready, 1)
                act.wait_ge(rs_ready, 3)
                act.activation(rs, rs, ACT.Exp, scale=-0.5).then_inc(rs_ready, 1)
                split(0)
                for k in range(KT):
                    act.wait_ge(scaled, k + 1)
                    act.copy(hn_hi[:, k, :], X[:, k, :]).then_inc(hi_done, 1)
                split(1)
                for k in range(KT):
                    wait_lo(act, k)
                act.wait_ge(hi_done, KT)
                act.copy(meta_hi[:, :, 0:META], hn_hi[:, :, SEQ:L].bitcast(F32)).then_inc(padded, 1)
                act.copy(meta_lo[:, :, 0:META], hn_lo[:, :, SEQ:L].bitcast(F32)).then_inc(padded, 1)
                for n, (part, tile) in enumerate(units):
                    rows = P if tile < TT else META
                    act.wait_ge(v_done, n + 1)
                    if n >= 2:
                        act.wait_ge(v_out[n % 2], 16 * (n // 2))
                    act.copy(stage[n % 2][0:rows, :], bank[(3 + n) % BANKS][0:rows, 0:QUARTER]).then_inc(v_copied, 1)
                    if tile == TT and part < 2:
                        split(part + 2)
                    if (part, tile) == (3, 2):
                        act.wait_ge(v_done, (TT + 1) * 3)
                        for i in range(2):
                            act.wait_ge(block_in[i].sem, 16)
                            act.copy(block_hi[i], block_raw[i]).then_inc(block_hi_done.sem, 1)
                act.wait_ge(lb_diff, 1)
                act.activation(t.lb[:], logits[:, 0, :], ACT.Sigmoid).then_inc(lb_sig, 1)

            @block.vector
            def _(dve):
                for k in range(1, KT):
                    dve.wait_ge(squared, k + 1)
                    if k > 1:
                        dve.wait_ge(added, k - 1)
                    dve.tensor_tensor(square_sum, square[0] if k == 1 else square_sum, square[k % 2],
                                      ALU.add).then_inc(added, 1)
                dve.wait_ge(lb_in, 16)
                dve.tensor_tensor(logits[:, 0, :], logits[:, 0, :], logits[:, 1, :],
                                  ALU.subtract).then_inc(lb_diff, 1)
                dve.wait_ge(rs_ready, 4)
                dve.wait_ge(consts_in, 32)
                for k in range(KT + 1):
                    if k < KT:
                        dve.scalar_tensor_tensor(out=X[:, k, :], in0=X[:, k, :], scalar=t.gain("mix_pre", k),
                                                 in1=rs, op0=ALU.mult, op1=ALU.mult).then_inc(scaled, 1)
                    if k and k - 1 in LO_BY_DVE:
                        make_lo(dve, k - 1)
                dve.wait_ge(lb_sig, 1)
                dve.tensor_scalar(t.omlb[:], t.lb[:], -1.0, 1.0, ALU.mult, ALU.add)
                dve.tensor_scalar(t.momlb[:], t.lb[:], 1.0, -1.0, ALU.mult, ALU.add)

            @block.gpsimd
            def _(pool):
                def weight_lo(part):
                    i = part % 2
                    pool.wait_ge(vw_hi_done, part + 1)
                    pool.tensor_tensor(vw_lo[i], vw_raw[i], vw_hi[i].bitcast(F32), ALU.subtract
                                       ).then_inc(vw_lo_done, 1)

                pool.memset(meta_hi[:, :, META:].bitcast(F32), 0.0).then_inc(padded, 1)
                pool.memset(meta_lo[:, :, META:].bitcast(F32), 0.0).then_inc(padded, 1)
                weight_lo(0)
                for k in LO_BY_POOL:
                    make_lo(pool, k)
                for part in range(1, 4):
                    weight_lo(part)
                for i in range(2):
                    pool.wait_ge(block_hi_done.sem, i + 1)
                    pool.tensor_tensor(block_lo[i], block_raw[i], block_hi[i].bitcast(F32), ALU.subtract
                                       ).then_inc(block_lo_done.sem, 1)

            @block.tensor
            def _(pe):
                pe.wait_ge(consts_in, 32)
                pe.wait_ge(added, KT - 1)
                for i, (a, n) in enumerate(CHUNKS3):
                    last = pe.matmul(bank[i][:, 0:n], t.const("ones"), square_sum[:, a:a + n], start=True, stop=True)
                last.then_inc(summed, 1)

                def step(n, k):
                    part, tile = units[n]
                    cols = slice(tile * P, (tile + 1) * P)
                    x_hi = hn_hi[:, k, cols] if tile < TT else meta_hi[:, k, :]
                    x_lo = hn_lo[:, k, cols] if tile < TT else meta_lo[:, k, :]
                    return three(pe, bank[(3 + n) % BANKS][:, 0:QUARTER], x_hi, x_lo, vw_hi[part % 2][:, k, :],
                                 vw_lo[part % 2][:, k, :], k == 0, k == KT - 1)

                pe.wait_ge(vw_lo_done, 1)
                pe.wait_ge(rs_ready, 3)
                for k in range(KT):
                    wait_lo(pe, k)
                    for n in range(BANKS):
                        last = step(n, k)
                        if k == KT - 1:
                            last.then_inc(v_done, 1)
                pe.wait_ge(padded, 4)
                for n in range(BANKS, len(units)):
                    if units[n][1] == 0:
                        pe.wait_ge(vw_lo_done, units[n][0] + 1)
                    pe.wait_ge(v_copied, n + 1 - BANKS)
                    for k in range(KT):
                        last = step(n, k)
                    last.then_inc(v_done, 1)


FWD, BWD = 0, 1
LATENTS = [("ckv", 0), ("cq", 0), ("cq", 1), ("cq", 2), ("ckv", 1), ("kr", 0)]


class Projections:

    def __init__(self, chunks, banks):
        self.chunks, self.banks = chunks, banks
        self.after = [sum(len(x) for x in chunks[:s + 1]) for s in range(6)]

    def first(self, s):
        return self.after[s] - len(self.chunks[s])


OF_HEAD = Projections([CHUNKS3 if n == "ff" else CHUNKS2 for n in IN_HGRN], [0, 1, 2] * 4 + [1])
OF_LATENTS = Projections([CHUNKS2 if n == "cq" else CHUNKS3 for n, _ in LATENTS], [0, 1, 2] * 5)
N_PROJ = OF_HEAD.after[-1]


def projections(p):
    return OF_LATENTS if p.j is None and p.base == HEADS else OF_HEAD


PE_STEPS = [(13, "turn", 0), (14, "turn", 1), (14, "updates", 0), (15, "turn", 2), (16, "updates", 1),
            (16, "turn", 3), (17, "turn", 4), (17, "updates", 2), (20, "updates", 3), (23, "updates", 4),
            (26, "near", 0), (29, "far", 0), (29, "near", 1), (30, "far", 1), (32, "outputs", 0),
            (39, "near", 2), (39, "far", 2), (41, "norm_sum", 0), (42, "near", 3), (42, "far", 3),
            (44, "outputs", 1), (45, "norm_sum", 1)]
ACT_STEPS = [("weight", 1), ("sigmoids", 0), ("copy", 0), ("weight", 2), ("ends_exp", 0), ("ends_exp", 1),
             ("ends_copy", 0), ("ends_copy", 1), ("copy", 1), ("ends_copy", 2), ("ends_copy", 3),
             ("ends_copy", 4), ("weight", 3), ("factors_exp", 0), ("copy", 2), ("factors_exp", 1),
             ("weight", 4), ("copy", 3), ("factors_exp", 2), ("weight", 5), ("factors_exp", 3),
             ("norm_square", 0), ("copy", 4), ("weight", 6), ("norm_rs", 0), ("norm_square", 1),
             ("norm_rs", 1), ("copy", 5)]
DVE_STEPS = [("queries", 0), ("keys", 0), ("gates", 0), ("sums", 0), ("sums", 1), ("ends_subtract", 0),
             ("ends_subtract", 1), ("keys", 1), ("ends_multiply", 0), ("states", 0), ("ends_multiply", 1),
             ("states", 1), ("factors_subtract", 0), ("factors_subtract", 1), ("states", 2), ("states", 3),
             ("factors_multiply", 0), ("states", 4), ("factors_multiply", 1), ("keep", 0), ("keep", 1),
             ("factors_subtract", 2), ("factors_subtract", 3), ("factors_multiply", 2),
             ("factors_multiply", 3), ("keep", 2), ("output", 0), ("keep", 3), ("output", 1)]


def spans(buf, lo, n, length, second):
    a = buf[:, lo:lo + n * length].rearrange("p (n h l) -> p n h l", n=n, h=2)
    return a[:, :, 1 if second else 0, :]


def hgrn_heads(nc, t, hn_hi, hn_lo, weights):
    with ExitStack() as c:
        def sb(name, shape, dt=F32):
            return c.enter_context(nc.sbuf_tensor(name, shape, dt))

        w_raw, w_hi, w_lo, w_in, w_hi_done, w_lo_done = weights.of_blocks()
        raw = {n: t.raw[:, s * L:s * L + (L if n == "ff" else SEQ)] for s, n in enumerate(IN_HGRN)}
        scan_mask = sb("scan_mask", [P, 2, L], mybir.dt.uint8)
        cum = [sb("cum_f", [P, L]), sb("cum_b", [P, SEQ])]
        sub = [sb("sub_f", [P, L]), sb("sub_b", [P, SEQ])]
        key = [sb("key_f", [P, L]), sb("key_b", [P, SEQ])]
        q, gate = sb("q", [P, SEQ]), sb("gate", [P, SEQ])
        FACTORS = 6 * HALF
        factor = [sb("factor_f", [P, FACTORS]), sb("factor_b", [P, FACTORS])]
        ends = [factor[d][:, 0:L if d == FWD else SEQ] for d in (FWD, BWD)]
        decay = [sb(f"decay{d}", [P, NCH]) for d in (FWD, BWD)]
        ends_t = [sb(f"ends_t{d}", [P, NCH, P]) for d in (FWD, BWD)]
        ends_meta_t = sb("ends_meta_t", [META, P])
        state = [sb(f"state{d}", [P, NCH, P]) for d in (FWD, BWD)]
        scores, diagonal = sb("scores", [P, GC, P]), sb("diagonal", [P, GC, P])
        values = sb("values_h", [P, TT + 1, P])
        square = sb("o_square", [P, HALF])
        rs = square
        r = sb("r", [P, HALF])
        waited = sb("waited", [P, 1])
        bank = [c.enter_context(nc.psum_tensor(f"h_bank{i}", [P, HALF], F32)) for i in range(8)]
        ends_bank, near_bank, far_bank, o_bank, u_bank = bank[3:8]

        def signal(name, per):
            return Signal(t.sem(name), per)

        proj_done, proj_copied = signal("proj_done", N_PROJ), signal("proj_copied", N_PROJ)
        v_in = signal("v_in", 32)
        sig_done, g_done = signal("sig_done", 6), signal("g_done", 2)
        key_done, q_done, gate_done, sums_done = (signal("key_done", 2), signal("q_done", 1),
                                                  signal("gate_done", 2), signal("sums_done", 4))
        ends_dif, ends_exp, ends_done = signal("ends_dif", 2), signal("ends_exp", 4), signal("ends_done", 2)
        ends_turned, ends_copied = signal("ends_turned", 5), signal("ends_copied", 5)
        u_done, state_done = signal("u_done", 5), signal("state_done", 15)
        fac_dif, fac_exp, fac_done = signal("fac_dif", 4), signal("fac_exp", 4), signal("fac_done", 4)
        near_done, far_done = signal("near_done", 4), signal("far_done", 4)
        near_kept, far_kept, scores_done = signal("near_kept", 4), signal("far_kept", 4), signal("scores_done", 2)
        o_done, o_squared, o_summed = signal("o_done", 2), signal("o_squared", 2), signal("o_summed", 2)
        rs_done, r_done, r_out, ga_out = (signal("o_rs_done", 4), signal("r_done", 4), signal("r_out", 32),
                                          signal("ga_out", 16))
        zeroed, masks_filled, masks_made = t.sem("zeroed"), t.sem("masks_filled"), t.sem("masks_made")

        def iterations(eng, both):
            both(At(0), None)
            both(At(1), At(0))
            with eng.Fori(0, HEADS - 2) as j:
                both(At(2, j), At(1, j))
            both(At(HEADS), At(HEADS - 1))

        def more(p, s):
            if p.j is None and p.base == 0 and s < 2:
                return False
            return s < 6 or p.j is not None or p.base < HEADS

        TURNS = [(FWD, 0), (FWD, 1), (BWD, 1), (BWD, 0)]
        GROUPS = [(FWD, 0), (BWD, 0), (FWD, 1), (BWD, 1)]
        STATE_AFTER = [1, 5, 8, 12, 15]

        def place(dd, name):
            a = {"q64": 0, "k64": 256, "q128": 512, "k128": 768, "q16": 1024, "k16": 1536, "q0": 2048,
                 "k32": 2560}[name]
            n = 256 if name in ("q64", "k64", "q128", "k128") else HALF
            return factor[dd][:, a:a + n]

        def in_time(dd, ap):
            return ap if dd == FWD else ap[:, ::-1]

        with nc.Block() as block:
            @block.sync
            def _(sp):
                def load(p, s):
                    w_hi_done.wait(sp, p, s - 1)
                    w_lo_done.wait(sp, p, s - 1)
                    sp.dma_start(w_raw[s % 2][:], dram_block(t.d["w_hgrn"], p.index() * 6 + s)
                                 ).then_inc(w_in[s % 2].sem, 16)

                def both(p, h):
                    for s in range(6):
                        if more(p, s + 1):
                            load(p, s + 1)
                        if h is not None and s == 1:
                            if h.j is not None or h.base:
                                store_r(h, 1, lag=1)
                            o_done.wait(sp, h, 2, lag=1)
                            hi = h.index()
                            sp.dma_start(values[:, 0:TT, :], t.d_v[:, 0:TT, bass.ts(hi, P)]).then_inc(v_in.sem, 16)
                            sp.dma_start(values[0:META, TT, :],
                                         t.d_v[0:META, TT, bass.ts(hi, P)]).then_inc(v_in.sem, 16)
                            sig_done.wait(sp, h, 6)
                            sp.dma_start(dram_head(t.d_ga, hi), raw["ga"][:]).then_inc(ga_out.sem, 16)
                        if h is not None and s == 5:
                            store_r(h, 0)

                def store_r(h, g, lag=0):
                    r_done.wait(sp, h, 2 * g + 2, lag)
                    sp.dma_start(dram_head(t.d_r, h.index() - lag)[:, g * HALF:(g + 1) * HALF],
                                 r[:]).then_inc(r_out.sem, 16)

                iterations(sp, both)
                store_r(At(HEADS - 1), 1)
                sp.wait_ge(r_out.sem, 32 * HEADS)
                sp.wait_ge(ga_out.sem, 16 * HEADS)

            @block.gpsimd
            def _(pool):
                pool.memset(scan_mask[:], 1).then_inc(masks_filled, 1)
                pool.wait_ge(masks_filled, 1)
                pool.memset(scan_mask[:, 0, ::CH], 0).then_inc(masks_made, 1)
                pool.memset(scan_mask[:, 1, ::SUB], 0).then_inc(masks_made, 1)
                for dd in (FWD, BWD):
                    pool.memset(place(dd, "k32"), 0.0).then_inc(zeroed, 1)
                pool.memset(diagonal[:], 0.0).then_inc(zeroed, 1)
                pool.memset(state[BWD][:, NCH - 1, :], 0.0).then_inc(zeroed, 1)

                def weight_lo(p, s):
                    w_hi_done.wait(pool, p, s + 1)
                    pool.tensor_tensor(w_lo[s % 2][:], w_raw[s % 2][:], w_hi[s % 2][:].bitcast(F32),
                                       ALU.subtract).then_inc(w_lo_done.sem, 1)

                def both(p, h):
                    for s in range(1, 7):
                        if more(p, s):
                            weight_lo(p, s)

                iterations(pool, both)

            @block.scalar
            def _(act):
                def sigmoids(h, _):
                    proj_copied.wait(act, h, N_PROJ)
                    q_done.wait(act, h, 1, lag=1)
                    far_kept.wait(act, h, 4, lag=1)
                    r_done.wait(act, h, 4, lag=1)
                    for n in IN_HGRN:
                        dst = {"q": q, "hg": gate}.get(n, raw[n])
                        act.activation(dst[:], raw[n][:], ACT.Sigmoid).then_inc(sig_done.sem, 1)
                    act.preload_act_table_set("natural_log_exp_and_others")
                    for dd, n in ((FWD, "ff"), (BWD, "fb")):
                        sig_done.wait(act, h, dd + 1)
                        hh = h.index() + dd * HEADS
                        act.activation(sub[dd][:], raw[n][:], ACT.Ln, bias=t.lb[:, bass.ds(hh, 1)],
                                       scale=t.omlb[:, bass.ds(hh, 1)]).then_inc(g_done.sem, 1)

                def ends_act(h, dd):
                    ends_dif.wait(act, h, dd + 1)
                    edge = cum[dd][:, CH - 1:SEQ:CH] if dd == FWD else cum[dd][:, 0:SEQ:CH]
                    act.activation(decay[dd][:], edge, ACT.Exp).then_inc(ends_exp.sem, 1)
                    act.activation(ends[dd], ends[dd], ACT.Exp).then_inc(ends_exp.sem, 1)

                def ends_copy(h, i):
                    ends_turned.wait(act, h, i + 1)
                    if i == 0:
                        act.copy(ends_meta_t[:], ends_bank[0:META, 0:P]).then_inc(ends_copied.sem, 1)
                        return
                    dd, g = TURNS[i - 1]
                    act.copy(ends_t[dd][:, g * GC:(g + 1) * GC, :],
                             ends_bank[:].rearrange("p (u d) -> p u d", u=GC)).then_inc(ends_copied.sem, 1)

                def factors_act(h, i):
                    dd, g = GROUPS[i]
                    fac_dif.wait(act, h, i + 1)
                    lo = g * HALF
                    act.activation(factor[dd][:, 0:1024], factor[dd][:, 0:1024], ACT.Exp)
                    k32 = spans(place(dd, "k32"), 0, HALF // 32, 32, dd == BWD)
                    act.activation(k32, k32, ACT.Exp)
                    act.activation(place(dd, "q16"), sub[dd][:, lo:lo + HALF], ACT.Exp)
                    act.activation(place(dd, "k16"), sub[dd][:, lo:lo + HALF], ACT.Exp, scale=-1.0)
                    act.activation(place(dd, "q0"), cum[dd][:, lo:lo + HALF], ACT.Exp).then_inc(fac_exp.sem, 1)

                def norm_square(h, g):
                    o_done.wait(act, h, g + 1)
                    if g:
                        r_done.wait(act, h, 2)
                    else:
                        r_done.wait(act, h, 4, lag=1)
                    act.activation(square[:], o_bank[:], ACT.Square).then_inc(o_squared.sem, 1)

                def norm_rs(h, g):
                    o_summed.wait(act, h, g + 1)
                    act.activation(rs[:], u_bank[:], ACT.Ln, bias=t.gain("eps", 0),
                                   scale=1.0 / P).then_inc(rs_done.sem, 1)
                    rs_done.wait(act, h, 2 * g + 1)
                    act.activation(rs[:], rs[:], ACT.Exp, scale=-0.5).then_inc(rs_done.sem, 1)

                def weight_hi(p, s):
                    w_in[s % 2].wait(act, p, 16 * (s // 2 + 1))
                    proj_done.wait(act, p, projections(p).after[s - 2] if s >= 2 else 0)
                    act.copy(w_hi[s % 2][:], w_raw[s % 2][:]).then_inc(w_hi_done.sem, 1)

                def copy_projection(p, h, s):
                    n = IN_HGRN[s]
                    if h is not None:
                        if n in ("ff", "fb"):
                            key_done.wait(act, h, 1 + (n == "fb"))
                            g_done.wait(act, h, 1 + (n == "fb"))
                        elif n == "q":
                            q_done.wait(act, h, 1)
                        elif n in ("hg", "gh"):
                            gate_done.wait(act, h, 2)
                        else:
                            ga_out.wait(act, h, 16)
                    made = projections(p)
                    for i, (a, w) in enumerate(made.chunks[s]):
                        e = made.first(s) + i
                        proj_done.wait(act, p, e + 1)
                        act.copy(t.raw[:, s * L + a:s * L + a + w],
                                 bank[made.banks[e]][:, 0:w]).then_inc(proj_copied.sem, 1)

                steps = {"sigmoids": sigmoids, "ends_exp": ends_act, "ends_copy": ends_copy,
                         "factors_exp": factors_act, "norm_square": norm_square, "norm_rs": norm_rs}

                def both(p, h):
                    for name, i in ACT_STEPS:
                        if name == "copy":
                            copy_projection(p, h, i)
                        elif name == "weight":
                            if more(p, i):
                                weight_hi(p, i)
                        elif h is not None:
                            steps[name](h, i)

                iterations(act, both)

            @block.vector
            def _(dve):
                def keys(h, dd):
                    sig_done.wait(dve, h, dd + 1)
                    hh = h.index() + dd * HEADS
                    dve.tensor_scalar(key[dd][:], raw["ff" if dd == FWD else "fb"][:], t.momlb[:, bass.ds(hh, 1)],
                                      t.omlb[:, bass.ds(hh, 1)], ALU.mult, ALU.add).then_inc(key_done.sem, 1)

                def queries(h, _):
                    sig_done.wait(dve, h, 3)
                    dve.tensor_tensor(q[:], q[:], raw["q"][:], ALU.mult).then_inc(q_done.sem, 1)

                def gates(h, _):
                    sig_done.wait(dve, h, 5)
                    dve.tensor_tensor(gate[:], gate[:], raw["hg"][:], ALU.mult).then_inc(gate_done.sem, 1)
                    gate_done.wait(dve, h, 1)
                    dve.scalar_tensor_tensor(out=gate[:], in0=gate[:], scalar=t.gain("hgrn", 0), in1=raw["gh"][:],
                                             op0=ALU.mult, op1=ALU.mult).then_inc(gate_done.sem, 1)

                def sums(h, dd):
                    g_done.wait(dve, h, dd + 1)
                    width = L if dd == FWD else SEQ
                    dve.tensor_tensor_scan(in_time(dd, cum[dd][:]), scan_mask[:, 0, 0:width],
                                           in_time(dd, sub[dd][:]), 0.0, ALU.mult,
                                           ALU.add).then_inc(sums_done.sem, 1)
                    dve.tensor_tensor_scan(in_time(dd, sub[dd][:]), scan_mask[:, 1, 0:width],
                                           in_time(dd, sub[dd][:]), 0.0, ALU.mult,
                                           ALU.add).then_inc(sums_done.sem, 1)

                def ends_subtract(h, dd):
                    sums_done.wait(dve, h, 2 * dd + 1)
                    far_done.wait(dve, h, 3 + dd, lag=1)
                    o_done.wait(dve, h, 2, lag=1)
                    b = cum[dd][:, 0:SEQ].rearrange("p (c l) -> p c l", c=NCH)
                    edge = b[:, :, CH - 1:CH] if dd == FWD else b[:, :, 0:1]
                    if dd == FWD:
                        dve.tensor_tensor(ends[dd][:, SEQ:L], cum[dd][:, L - 1:L].to_broadcast([P, META]),
                                          cum[dd][:, SEQ:L], ALU.subtract)
                    dve.tensor_tensor(ends[dd][:, 0:SEQ].rearrange("p (c l) -> p c l", c=NCH),
                                      edge.to_broadcast([P, NCH, CH]), b, ALU.subtract).then_inc(ends_dif.sem, 1)

                def ends_multiply(h, dd):
                    key_done.wait(dve, h, dd + 1)
                    ends_exp.wait(dve, h, 2 * dd + 2)
                    dve.tensor_tensor(ends[dd], ends[dd], key[dd][:], ALU.mult).then_inc(ends_done.sem, 1)

                def factors_subtract(h, i):
                    dd, g = GROUPS[i]
                    if g == 0:
                        ends_turned.wait(dve, h, 3 if dd == FWD else 5)
                    else:
                        far_done.wait(dve, h, i - 1)
                        o_done.wait(dve, h, 1)
                    lo = g * HALF
                    sums_done.wait(dve, h, 2 * dd + 2)
                    for span, names in ((64, ("q64", "k64")), (128, ("q128", "k128")), (32, (None, "k32"))):
                        n = HALF // span
                        b = cum[dd][:, lo:lo + HALF].rearrange("p (n l) -> p n l", n=n)
                        ref = span // 2 - 1 if dd == FWD else span // 2
                        refs = b[:, :, ref:ref + 1].to_broadcast([P, n, span // 2])
                        queries = spans(cum[dd], lo, n, span, dd == FWD)
                        keys = spans(cum[dd], lo, n, span, dd == BWD)
                        if names[0]:
                            dve.tensor_tensor(place(dd, names[0]).rearrange("p (n l) -> p n l", n=n), queries,
                                              refs, ALU.subtract)
                            dst = place(dd, names[1]).rearrange("p (n l) -> p n l", n=n)
                        else:
                            dst = spans(place(dd, names[1]), 0, n, span, dd == BWD)
                        last = dve.tensor_tensor(dst, refs, keys, ALU.subtract)
                    last.then_inc(fac_dif.sem, 1)

                def factors_multiply(h, i):
                    dd, g = GROUPS[i]
                    lo = g * HALF
                    fac_exp.wait(dve, h, i + 1)
                    q_done.wait(dve, h, 1)
                    for name, src in (("q16", q), ("k16", key[dd]), ("q0", q)):
                        dve.tensor_tensor(place(dd, name), place(dd, name), src[:, lo:lo + HALF], ALU.mult)
                    for span in (64, 128):
                        n = HALF // span
                        for name, src, second in ((f"q{span}", q, dd == FWD), (f"k{span}", key[dd], dd == BWD)):
                            dst = place(dd, name).rearrange("p (n l) -> p n l", n=n)
                            dve.tensor_tensor(dst, dst, spans(src, lo, n, span, second), ALU.mult)
                    k32 = spans(place(dd, "k32"), 0, HALF // 32, 32, dd == BWD)
                    dve.tensor_tensor(k32, k32, spans(key[dd], lo, HALF // 32, 32, dd == BWD),
                                      ALU.mult).then_inc(fac_done.sem, 1)

                def states(h, i):
                    u_done.wait(dve, h, i + 1)
                    o_done.wait(dve, h, 2, lag=1)
                    if i == 0:
                        dve.tensor_copy(state[FWD][:, 0, :], u_bank[:, 0:P]).then_inc(state_done.sem, 1)
                        return
                    dd, g = TURNS[i - 1]
                    us = range(GC) if dd == FWD else range(GC - 1, -1, -1)
                    event = STATE_AFTER[i - 1]
                    for u in us:
                        ch = g * GC + u
                        to = ch + 1 if dd == FWD else ch - 1
                        if not 0 <= to < NCH:
                            continue
                        if not (dd == BWD and ch == NCH - 1):
                            state_done.wait(dve, h, event)
                        dve.scalar_tensor_tensor(out=state[dd][:, to, :], in0=state[dd][:, ch, :],
                                                 scalar=decay[dd][:, ch:ch + 1], in1=u_bank[:, u * P:(u + 1) * P],
                                                 op0=ALU.mult, op1=ALU.add).then_inc(state_done.sem, 1)
                        event += 1
                    assert event == STATE_AFTER[i]

                def keep(h, i):
                    dd, g = GROUPS[i]
                    side = "f" if dd == FWD else "b"
                    if g == 0:
                        o_done.wait(dve, h, 2, lag=1)
                    else:
                        o_done.wait(dve, h, 1)
                    for name, done, kept, src in (("near", near_done, near_kept, near_bank),
                                                  ("far", far_done, far_kept, far_bank)):
                        done.wait(dve, h, i + 1)
                        if name == "far":
                            near_kept.wait(dve, h, i + 1)
                        else:
                            far_kept.wait(dve, h, *((i, 0) if i else (4, 1)))
                        if name == "near" and dd == BWD:
                            scores_done.wait(dve, h, *((1, 0) if g else (2, 1)))
                        dve.memset(waited[:], 0.0)
                        src = src[:].rearrange("p (u t) -> p u t", u=GC)
                        last = keep_where(f"mask_{side}_{name}", scores, src)
                        if name == "near" and dd == BWD:
                            last = keep_where("ident", diagonal, src)
                        last.then_inc(kept.sem, 1)
                    if dd == BWD:
                        far_kept.wait(dve, h, i + 1)
                        dve.tensor_tensor(scores[:], scores[:], diagonal[:], ALU.add).then_inc(scores_done.sem, 1)

                def keep_where(mask, dst, src):
                    mask = t.const(mask).bitcast(U32)
                    return dve.copy_predicated(dst[:], mask.unsqueeze(1).to_broadcast([P, GC, P]), src)

                def output(h, g):
                    rs_done.wait(dve, h, 2 * g + 2)
                    if g:
                        r_out.wait(dve, h, 16)
                    else:
                        r_out.wait(dve, h, 32, lag=1)
                    dve.tensor_tensor(r[:], o_bank[:], rs[:], ALU.mult).then_inc(r_done.sem, 1)
                    r_done.wait(dve, h, 2 * g + 1)
                    dve.tensor_tensor(r[:], r[:], gate[:, g * HALF:(g + 1) * HALF], ALU.mult
                                      ).then_inc(r_done.sem, 1)

                dve.wait_ge(masks_made, 2)
                dve.wait_ge(zeroed, 4)

                steps = {"keys": keys, "queries": queries, "gates": gates, "sums": sums, "ends_subtract": ends_subtract, "ends_multiply": ends_multiply,
                         "factors_subtract": factors_subtract, "factors_multiply": factors_multiply,
                         "states": states, "keep": keep, "output": output}

                def both(p, h):
                    if h is not None:
                        for name, i in DVE_STEPS:
                            steps[name](h, i)

                iterations(dve, both)

            @block.tensor
            def _(pe):
                def turn(h, i):
                    if i == 0:
                        ends_done.wait(pe, h, 1)
                        ends_copied.wait(pe, h, 5, lag=1)
                        pe.matmul(ends_bank[0:META, 0:P], ends[FWD][:, SEQ:L], t.const("ident"), start=True,
                                  stop=True).then_inc(ends_turned.sem, 1)
                        return
                    dd, g = TURNS[i - 1]
                    ends_done.wait(pe, h, dd + 1)
                    ends_copied.wait(pe, h, i)
                    for u in range(GC):
                        a = (g * GC + u) * CH
                        last = pe.transpose(ends_bank[:, u * P:(u + 1) * P], ends[dd][:, a:a + CH],
                                            t.const("ident"))
                    last.then_inc(ends_turned.sem, 1)

                def updates(h, i):
                    ends_copied.wait(pe, h, i + 1)
                    if i == 0:
                        v_in.wait(pe, h, 32)
                        rs_done.wait(pe, h, 4, lag=1)
                        pe.matmul(u_bank[:, 0:P], ends_meta_t[:], values[0:META, TT, :], start=True,
                                  stop=True).then_inc(u_done.sem, 1)
                        return
                    dd, g = TURNS[i - 1]
                    state_done.wait(pe, h, STATE_AFTER[i - 1])
                    for u in range(GC):
                        ch = g * GC + u
                        last = pe.matmul(u_bank[:, u * P:(u + 1) * P], ends_t[dd][:, ch, :], values[:, ch, :],
                                         start=True, stop=True)
                    last.then_inc(u_done.sem, 1)

                def near(h, i):
                    dd, g = GROUPS[i]
                    fac_done.wait(pe, h, i + 1)
                    if i:
                        near_kept.wait(pe, h, i)
                    else:
                        near_kept.wait(pe, h, 4, lag=1)
                    for u in range(GC):
                        a = slice(u * CH, (u + 1) * CH)
                        last = pe.matmul(near_bank[:, a], place(dd, "k16")[:, a], place(dd, "q16")[:, a],
                                         start=True, stop=True)
                    last.then_inc(near_done.sem, 1)

                def far(h, i):
                    dd, g = GROUPS[i]
                    if i:
                        far_kept.wait(pe, h, i)
                    else:
                        far_kept.wait(pe, h, 4, lag=1)
                    for u in range(GC):
                        a = slice(u * CH, (u + 1) * CH)
                        pe.matmul(far_bank[:, a], place(dd, "k32")[:, a], place(dd, "q16")[:, a], start=True,
                                  stop=True)
                        for span in (64, 128):
                            half = span // 2
                            for n in range(CH // span):
                                keys = n * span + (0 if dd == FWD else half)
                                queries = n * span + (half if dd == FWD else 0)
                                b = (u * (CH // span) + n) * half
                                last = pe.matmul(
                                    far_bank[keys:keys + half, u * CH + queries:u * CH + queries + half],
                                    place(dd, f"k{span}")[:, b:b + half], place(dd, f"q{span}")[:, b:b + half],
                                    start=True, stop=True)
                    last.then_inc(far_done.sem, 1)

                def outputs(h, g):
                    scores_done.wait(pe, h, g + 1)
                    state_done.wait(pe, h, 15)
                    if g:
                        r_done.wait(pe, h, 1)
                    else:
                        r_done.wait(pe, h, 3, lag=1)
                    for u in range(GC):
                        ch, a = g * GC + u, slice(u * CH, (u + 1) * CH)
                        pe.matmul(o_bank[:, a], values[:, ch, :], scores[:, u, :], start=True, stop=False)
                        for dd in (FWD, BWD):
                            last = pe.matmul(o_bank[:, a], state[dd][:, ch, :], place(dd, "q0")[:, a],
                                             start=False, stop=(dd == BWD))
                    last.then_inc(o_done.sem, 1)

                def norm_sum(h, g):
                    o_squared.wait(pe, h, g + 1)
                    if g:
                        rs_done.wait(pe, h, 1)
                    pe.matmul(u_bank[:], t.const("ones"), square[:], start=True, stop=True
                              ).then_inc(o_summed.sem, 1)

                def project(p, h, s):
                    made = projections(p)
                    w_lo_done.wait(pe, p, s + 1)
                    for i in range(len(made.chunks[s])):
                        e = made.first(s) + i
                        same = [x for x in range(e) if made.banks[x] == made.banks[e]]
                        if same:
                            proj_copied.wait(pe, p, same[-1] + 1)
                        else:
                            last_use = max(x for x in range(N_PROJ) if OF_HEAD.banks[x] == made.banks[e])
                            proj_copied.wait(pe, p, last_use + 1, lag=1)
                    for k in range(KT):
                        for i, (a, w) in enumerate(made.chunks[s]):
                            out = bank[made.banks[made.first(s) + i]][:, 0:w]
                            xh, xl = hn_hi[:, k, a:a + w], hn_lo[:, k, a:a + w]
                            last = three(pe, out, w_hi[s % 2][:, k, :], w_lo[s % 2][:, k, :], xh, xl, k == 0,
                                         k == KT - 1)
                            if k == KT - 1:
                                last.then_inc(proj_done.sem, 1)
                        if h is not None:
                            for at, name, i in PE_STEPS:
                                if at == s * KT + k:
                                    steps[name](h, i)

                steps = {"turn": turn, "updates": updates, "near": near, "far": far, "outputs": outputs,
                         "norm_sum": norm_sum}

                def both(p, h):
                    if h is not None and h.j is None and h.base == 0:
                        pe.wait_ge(zeroed, 4)
                    for s in range(6):
                        project(p, h, s)

                iterations(pe, both)


def dram_head(x, i):
    return x[bass.ds(i, 1)].rearrange("a p n -> (a p) n")


def dram_block(x, i):
    return x[bass.ds(i, 1)].rearrange("a p k m -> (a p) k m")


LK = (TT + 1) * P


class Latents:

    def __init__(self, t, weights, memory, semaphores):
        def sb(name, shape, dt=F32):
            return memory.enter_context(t.nc.sbuf_tensor(name, shape, dt))

        def signal(name, per):
            return Signal(semaphores.enter_context(t.nc.semaphore(name)), per)

        self.parts = {(n, x): sb(f"{n}_{x}", [P, k, w], F32R)
                      for n, k, w in (("cq", QT, SEQ), ("ckv", KVT, LK), ("kr", 1, LK)) for x in ("hi", "lo")}
        self.table = sb("rope_table", [P, L])
        self.weights = (*(x[0] for x in weights.blocks()),
                        signal("aw_in", 16), signal("aw_hi_done", 1), signal("aw_lo_done", 1))


def latents(nc, t, lat):
    with ExitStack() as c:
        def sb(name, shape, dt=F32):
            return c.enter_context(nc.sbuf_tensor(name, shape, dt))

        w_raw = [sb(f"lw_raw{i}", [P, KVT, HALF]) for i in range(2)]
        w_hi = [sb(f"lw_hi{i}", [P, KVT, HALF], F32R) for i in range(2)]
        w_lo = [sb(f"lw_lo{i}", [P, KVT, HALF], F32R) for i in range(2)]
        aw_raw, aw_hi, aw_lo, aw_in, aw_hi_done, aw_lo_done = lat.weights
        TILES = [("ckv", 0), ("ckv", 1), ("cq", 0), ("cq", 1), ("cq", 2)]
        width = {"ckv": L, "cq": SEQ, "kr": L}
        chunks = {"ckv": CHUNKS3, "cq": CHUNKS2}
        raw = {x: t.raw[:, s * L:s * L + width[x[0]]] for s, x in enumerate(LATENTS)}
        square = {x: sb(f"l_square_{x[0]}{x[1]}", [P, width[x[0]]]) for x in TILES}
        rs = {n: sb(f"rs_{n}", [P, width[n]]) for n in ("ckv", "cq")}
        hi = {n: lat.parts[n, "hi"] for n in width}
        lo = {n: lat.parts[n, "lo"] for n in width}
        turned = sb("kr_turned", [P, L])
        stage = [sb(f"mv_stage{i}", [P, HALF]) for i in range(2)]
        bank = [c.enter_context(nc.psum_tensor(f"l_bank{i}", [P, HALF], F32)) for i in range(8)]
        sum_banks = {"cq": bank[3:5], "ckv": bank[5:8]}
        sem = t.sem
        w_in, table_in = [sem(f"lw_in{i}") for i in range(2)], sem("table_in")
        w_hi_done, w_lo_done = sem("lw_hi_done"), sem("lw_lo_done")
        squared = {x: sem(f"squared_{x[0]}{x[1]}") for x in TILES}
        summed = {n: sem(f"summed_{n}") for n in rs}
        rs_done = {n: sem(f"rs_done_{n}") for n in rs}
        scaled, hi_done, lo_done = ([{n: sem(f"{e}_{n}") for n in width} for e in ("scaled", "hi_done", "lo_done")])
        turned_done, folded, padded = sem("kr_turned_done"), sem("kr_folded"), sem("latents_padded")
        v_done, v_copied = sem("mv_done"), sem("mv_copied")
        v_out = [sem(f"mv_out{i}") for i in range(2)]
        units = [(half, tile) for half in range(2) for tile in range(TT + 1)]
        BY_DVE = [("ckv", 1), ("cq", 2)]

        with nc.Block() as block:
            @block.sync
            def _(sp):
                sp.dma_start(w_raw[0][:], t.d["w_v"][0]).then_inc(w_in[0], 16)
                sp.dma_start(lat.table[:], t.d["rope"]).then_inc(table_in, 16)
                sp.dma_start(w_raw[1][:], t.d["w_v"][1]).then_inc(w_in[1], 16)
                sp.dma_start(aw_raw[:], t.d["w_head"][0]).then_inc(aw_in.sem, 16)
                for n, (half, tile) in enumerate(units):
                    rows = P if tile < TT else META
                    sp.wait_ge(v_copied, n + 1)
                    sp.dma_start(t.d_mv[0:rows, tile, half * HALF:(half + 1) * HALF],
                                 stage[n % 2][0:rows, :]).then_inc(v_out[n % 2], 16)
                for i in range(2):
                    sp.wait_ge(v_out[i], 16 * (len(units) // 2))

            @block.gpsimd
            def _(pool):
                for n in ("ckv", "kr"):
                    for part in (hi[n], lo[n]):
                        pool.memset(part[:, :, L:].bitcast(F32), 0.0).then_inc(padded, 1)
                for b in range(2):
                    pool.wait_ge(w_hi_done, b + 1)
                    pool.tensor_tensor(w_lo[b][:], w_raw[b][:], w_hi[b][:].bitcast(F32),
                                       ALU.subtract).then_inc(w_lo_done, 1)
                pool.wait_ge(aw_hi_done.sem, 1)
                pool.tensor_tensor(aw_lo[:], aw_raw[:], aw_hi[:].bitcast(F32), ALU.subtract
                                   ).then_inc(aw_lo_done.sem, 1)

            @block.scalar
            def _(act):
                act.preload_act_table_set("natural_log_exp_and_others")

                def weight_hi(b):
                    act.wait_ge(w_in[b], 16)
                    act.copy(w_hi[b][:], w_raw[b][:]).then_inc(w_hi_done, 1)

                def rms(n, tiles):
                    act.wait_ge(summed[n], 1)
                    for i, (a, w) in enumerate(chunks[n]):
                        act.activation(rs[n][:, a:a + w], sum_banks[n][i][:, 0:w], ACT.Ln, bias=t.gain("eps", 0),
                                       scale=1.0 / (P * tiles)).then_inc(rs_done[n], 1)
                    act.wait_ge(rs_done[n], len(chunks[n]))
                    act.activation(rs[n][:], rs[n][:], ACT.Exp, scale=-0.5).then_inc(rs_done[n], 1)

                def latent_hi(n, i):
                    act.wait_ge(scaled[n], i + 1)
                    act.activation(hi[n][:, i, 0:width[n]], raw[n, i], ACT.Copy,
                                   scale=t.gain(n, i)).then_inc(hi_done[n], 1)

                def value_copy(u):
                    rows = P if units[u][1] < TT else META
                    act.wait_ge(v_done, u + 1)
                    if u >= 2:
                        act.wait_ge(v_out[u % 2], 16 * (u // 2))
                    act.copy(stage[u % 2][0:rows, :], bank[5 + u % 3][0:rows, :]).then_inc(v_copied, 1)

                for x in TILES:
                    if x not in BY_DVE:
                        act.activation(square[x][:], raw[x], ACT.Square).then_inc(squared[x], 1)
                    if x == ("ckv", 0):
                        weight_hi(0)
                rms("ckv", KVT)
                for i in range(KVT):
                    latent_hi("ckv", i)
                rms("cq", QT)
                for u in range(len(units)):
                    value_copy(u)
                    if u % 2 and u // 2 < QT:
                        latent_hi("cq", u // 2)
                    if u == 2:
                        weight_hi(1)
                    if u == 6:
                        for x, (a, w) in enumerate(CHUNKS3):
                            act.wait_ge(folded, x + 1)
                            act.copy(hi["kr"][:, 0, a:a + w], bank[x][:, 0:w]).then_inc(hi_done["kr"], 1)
                    if u == 8:
                        act.wait_ge(aw_in.sem, 16)
                        act.copy(aw_hi[:], aw_raw[:]).then_inc(aw_hi_done.sem, 1)

            @block.vector
            def _(dve):
                for x in BY_DVE:
                    dve.tensor_tensor(square[x][:], raw[x], raw[x], ALU.mult).then_inc(squared[x], 1)
                dve.wait_ge(table_in, 16)
                dve.tensor_tensor(turned[:], raw["kr", 0], lat.table[:], ALU.mult).then_inc(turned_done, 1)
                for n, tiles in (("ckv", KVT), ("cq", QT)):
                    dve.wait_ge(rs_done[n], len(chunks[n]) + 1)
                    for i in range(tiles):
                        dve.tensor_tensor(raw[n, i], raw[n, i], rs[n][:], ALU.mult).then_inc(scaled[n], 1)
                    for i in range(tiles):
                        dve.wait_ge(hi_done[n], i + 1)
                        dve.wait_ge(scaled[n], i + 1)
                        dve.scalar_tensor_tensor(out=lo[n][:, i, 0:width[n]], in0=raw[n, i], scalar=t.gain(n, i),
                                                 in1=hi[n][:, i, 0:width[n]].bitcast(F32), op0=ALU.mult,
                                                 op1=ALU.subtract).then_inc(lo_done[n], 1)
                for x, (a, w) in enumerate(CHUNKS3):
                    dve.wait_ge(hi_done["kr"], x + 1)
                    dve.tensor_tensor(lo["kr"][:, 0, a:a + w], bank[x][:, 0:w], hi["kr"][:, 0, a:a + w].bitcast(F32),
                                      ALU.subtract).then_inc(lo_done["kr"], 1)

            @block.tensor
            def _(pe):
                for n, tiles in (("ckv", KVT), ("cq", QT)):
                    for i in range(tiles):
                        pe.wait_ge(squared[n, i], 1)
                        for x, (a, w) in enumerate(chunks[n]):
                            last = pe.matmul(sum_banks[n][x][:, 0:w], t.const("ones"), square[n, i][:, a:a + w],
                                             start=(i == 0), stop=(i == tiles - 1))
                    last.then_inc(summed[n], 1)
                pe.wait_ge(turned_done, 1)
                for x, (a, w) in enumerate(CHUNKS3):
                    pe.matmul(bank[x][:, 0:w], t.const("fold"), turned[:, a:a + w], start=True,
                              stop=True).then_inc(folded, 1)
                pe.wait_ge(lo_done["ckv"], KVT)
                pe.wait_ge(padded, 4)
                pe.wait_ge(rs_done["ckv"], 4)
                for u, (half, tile) in enumerate(units):
                    if tile == 0:
                        pe.wait_ge(w_lo_done, half + 1)
                    if u >= 3:
                        pe.wait_ge(v_copied, u - 2)
                    cols = slice(tile * P, (tile + 1) * P)
                    for k in range(KVT):
                        last = three(pe, bank[5 + u % 3][:], hi["ckv"][:, k, cols], lo["ckv"][:, k, cols],
                                     w_hi[half][:, k, :], w_lo[half][:, k, :], k == 0, k == KVT - 1)
                    last.then_inc(v_done, 1)


def attention_heads(nc, t, weights, lat, used):
    with ExitStack() as c:
        def sb(name, shape, dt=F32):
            return c.enter_context(nc.sbuf_tensor(name, shape, dt))

        both_parts = ("hi", "lo")
        cq, ckv = ({x: lat.parts[n, x] for x in both_parts} for n in ("cq", "ckv"))
        kr = {x: lat.parts["kr", x][:, 0, :] for x in both_parts}
        table = lat.table
        w_raw, w_hi, w_lo, w_in, w_hi_done, w_lo_done = lat.weights
        q_nope = {(x, i): sb(f"q_nope_{x}{i}", [P, HALF], F32R) for x in both_parts for i in range(2)}
        gate, *rope_parts = weights.halves_of_second()
        q_rope = {(x, i): rope_parts[n][i] for n, x in enumerate(both_parts) for i in range(2)}
        q_turned = sb("q_turned", [P, HALF])
        k_nope = {(x, i): sb(f"k_nope_{x}{i}", [P, LK], F32R) for x in both_parts for i in range(2)}
        v_raw = t.raw[:, (TT + 1) * HALF:(TT + 1) * (HALF + P)].rearrange("p (k m) -> p k m", k=TT + 1)
        v = {(x, i): sb(f"v_{x}{i}", [P, TT + 1, P], F32R) for x in both_parts for i in range(2)}
        scores = [t.raw[:, 0:(TT + 1) * HALF].rearrange("p (k q) -> p k q", k=TT + 1), sb("s1", [P, TT + 1, HALF])]
        top = sb("running_max", [P, HALF])
        q_max = sb("q_max", [P, HALF // P])
        spread = sb("max_spread", [P, HALF])
        RING = 3
        prob = [sb(f"prob{i}", [P, HALF]) for i in range(RING)]
        prob_hi = [sb(f"prob_hi{i}", [P, HALF], F32R) for i in range(RING)]
        prob_lo = [sb(f"prob_lo{i}", [P, HALF], F32R) for i in range(RING)]
        prob_sum, inv = sb("prob_sum", [P, HALF]), sb("inv_sum", [P, HALF])
        rec = [sb(f"rec{i}", [P, HALF]) for i in range(2)]
        mixed = [sb(f"mixed{i}", [P, HALF]) for i in range(2)]
        bank = [c.enter_context(nc.psum_tensor(f"a_bank{i}", [P, HALF], F32)) for i in range(8)]
        s_bank, o_bank, max_bank, sum_bank = bank[0:2], [bank[2], bank[5]], bank[6], bank[7]
        TILES = TT + 1
        PIECES = [("k", 2 * QT, KVT, ckv, a, w, bank[3 + i % 2]) for i, (a, w) in enumerate(CHUNKS3)]
        for i in range(2):
            PIECES.append((f"nope{i}", 0, QT, cq, i * HALF, HALF, bank[4]))
            PIECES.append((f"rope{i}", QT, QT, cq, i * HALF, HALF, bank[3]))
        NP_ = len(PIECES)
        BEFORE = {}
        for i in range(NP_):
            same = [x for x in range(-NP_, i) if PIECES[x % NP_][6] is PIECES[i][6]]
            BEFORE[i] = same[-1] + 1

        def signal(name, per):
            return Signal(t.sem(name), per)

        zeroed = t.sem("k_padded")
        v_in, v_hi_done, v_lo_done = signal("av_in", 32), signal("av_hi_done", 2), signal("av_lo_done", 2)
        piece_done, piece_hi, piece_read = signal("a_piece", NP_), signal("a_piece_hi", NP_), signal("a_read", NP_)
        rope_lo = signal("rope_lo", 2)
        s_done, s_kept, top_done = signal("s_done", 2 * TILES), signal("s_kept", 2 * TILES), signal("top_done", 16)
        top_turned, q_max_done = signal("top_turned", 2), signal("q_max_done", 2)
        spread_done, spread_kept = signal("spread_done", 2), signal("spread_kept", 2)
        p_dif, p_exp, p_hi, p_lo = (signal("p_dif", 2 * TILES), signal("p_exp", 2 * TILES),
                                    signal("p_hi", 2 * TILES), signal("p_lo", 2 * TILES))
        p_sum, pv_done = signal("p_sum", 16), signal("pv_done", 2 * TILES)
        sum_done, inv_done = signal("sum_done", 2), signal("inv_done", 4)
        o_scaled, mix_done = signal("o_scaled", 2), signal("mix_done", 4)
        gate_in = [signal(f"gate_in{i}", 32) for i in range(2)]
        mixed_out = [signal(f"mixed_out{i}", 16) for i in range(2)]

        def rows(k):
            return P if k < TT else META

        def iterations(eng, both):
            both(At(0), None)
            both(At(1), At(0))
            with eng.Fori(0, HEADS // 2 - 1) as j:
                both(At(2, j, 2), At(1, j, 2))
                both(At(3, j, 2), At(2, j, 2))
            both(None, At(HEADS - 1))

        def segments(p, h):
            cur0, cur1 = ((h, 0), (h, 1)) if h is not None else (None, None)
            nxt1 = (p, 0) if p is not None else None
            return (cur0, cur1), (cur1, nxt1)

        with nc.Block() as block:
            @block.sync
            def _(sp):
                for s in used:
                    sp.sem_clear(s)

                def both(p, h):
                    if p is not None:
                        v_hi_done.wait(sp, p, 2, lag=1)
                        v_lo_done.wait(sp, p, 2, lag=1)
                        hp = p.index()
                        sp.dma_start(v_raw[:, 0:TT, :], t.d_mv[:, 0:TT, bass.ts(hp, P)]).then_inc(v_in.sem, 16)
                        sp.dma_start(v_raw[0:META, TT, :],
                                     t.d_mv[0:META, TT, bass.ts(hp, P)]).then_inc(v_in.sem, 16)
                    if h is not None:
                        hh = h.index()
                        for i in range(2):
                            mix_done.wait(sp, h, 2 * i + 2, lag=1)
                            cols = slice(i * HALF, (i + 1) * HALF)
                            sp.dma_start(gate[i][:], dram_head(t.d_ga, hh)[:, cols]).then_inc(gate_in[i].sem, 16)
                            sp.dma_start(rec[i][:], dram_head(t.d_r, hh)[:, cols]).then_inc(gate_in[i].sem, 16)
                    if p is not None:
                        w_hi_done.wait(sp, p, 1)
                        w_lo_done.wait(sp, p, 1)
                        sp.dma_start(w_raw[:], dram_block(t.d["w_head"], p.index() + 1)).then_inc(w_in.sem, 16)
                    if h is not None:
                        for i in range(2):
                            mix_done.wait(sp, h, 2 * i + 2)
                            sp.dma_start(dram_head(t.d_mixed, hh)[:, i * HALF:(i + 1) * HALF],
                                         mixed[i][:]).then_inc(mixed_out[i].sem, 16)

                iterations(sp, both)
                for i in range(2):
                    sp.wait_ge(mixed_out[i].sem, 16 * HEADS)

            @block.gpsimd
            def _(pool):
                for x in both_parts:
                    for i in range(2):
                        pool.memset(k_nope[x, i][:, L:].bitcast(F32), 0.0).then_inc(zeroed, 1)

                def weights(at, k):
                    w_hi_done.wait(pool, at, k)
                    pool.tensor_tensor(w_lo[:], w_raw[:], w_hi[:].bitcast(F32), ALU.subtract
                                       ).then_inc(w_lo_done.sem, 1)

                def rope_part(p, i):
                    piece_hi.wait(pool, p, 5 + 2 * i)
                    pool.tensor_tensor(q_rope["lo", i][:], q_turned[:], q_rope["hi", i][:].bitcast(F32),
                                       ALU.subtract).then_inc(rope_lo.sem, 1)

                def values(p):
                    par = p.base % 2
                    v_hi_done.wait(pool, p, 2)
                    pool.tensor_tensor(v["lo", par][:, 0:TT, :], v_raw[:, 0:TT, :],
                                       v["hi", par][:, 0:TT, :].bitcast(F32), ALU.subtract
                                       ).then_inc(v_lo_done.sem, 1)
                    pool.tensor_tensor(v["lo", par][0:META, TT, :], v_raw[0:META, TT, :],
                                       v["hi", par][0:META, TT, :].bitcast(F32), ALU.subtract
                                       ).then_inc(v_lo_done.sem, 1)

                def segment(cur, p, which):
                    for k in range(TILES):
                        if cur is not None and k:
                            h, i = cur
                            p_exp.wait(pool, h, i * TILES + k + 1)
                            n = rows(k)
                            if k == 1:
                                sum_done.wait(pool, h, i)
                                a, out = prob[0], prob_sum
                            else:
                                p_sum.wait(pool, h, i * 8 + k - 1)
                                a, out = prob_sum, prob_sum
                            pool.tensor_tensor(out[0:n, :], a[0:n, :], prob[k % RING][0:n, :], ALU.add
                                               ).then_inc(p_sum.sem, 1)
                        if k == 4 and p is not None:
                            if which == 0:
                                values(p)
                            else:
                                weights(p, 2)
                    if cur is not None:
                        h, i = cur
                        o_scaled.wait(pool, h, i + 1)
                        gate_in[i].wait(pool, h, 32)
                        pool.tensor_tensor(mixed[i][:], mixed[i][:], gate[i][:], ALU.mult
                                           ).then_inc(mix_done.sem, 1)
                        mix_done.wait(pool, h, 2 * i + 1)
                        pool.tensor_tensor(mixed[i][:], mixed[i][:], rec[i][:], ALU.add).then_inc(mix_done.sem, 1)

                def both(p, h):
                    for which, (cur, nxt) in enumerate(segments(p, h)):
                        if p is not None:
                            rope_part(p, which)
                        segment(cur, p, which)

                iterations(pool, both)

            @block.scalar
            def _(act):
                def weights(at, k):
                    w_in.wait(act, at, 16 * k)
                    piece_done.wait(act, at, NP_ * (k - 1))
                    act.copy(w_hi[:], w_raw[:]).then_inc(w_hi_done.sem, 1)

                def piece(p, i):
                    name, _, _, _, a, w, src = PIECES[i]
                    if name == "k":
                        par = p.base % 2
                        piece_done.wait(act, p, i + 1)
                        s_done.wait(act, p, 0, lag=1)
                        act.copy(k_nope["hi", par][:, a:a + w], src[:, 0:w]).then_inc(piece_hi.sem, 1)
                        return
                    half = int(name[-1])
                    s_done.wait(act, p, (half + 1) * TILES, lag=1)
                    if name.startswith("nope"):
                        piece_done.wait(act, p, i + 1)
                        act.copy(q_nope["hi", half][:], src[:]).then_inc(piece_hi.sem, 1)
                    else:
                        piece_read.wait(act, p, i + 1)
                        act.copy(q_rope["hi", half][:], q_turned[:]).then_inc(piece_hi.sem, 1)

                def spread_keep(h, i):
                    spread_done.wait(act, h, i + 1)
                    p_dif.wait(act, h, i * TILES)
                    act.copy(spread[:], max_bank[:]).then_inc(spread_kept.sem, 1)

                def values(p):
                    par = p.base % 2
                    v_in.wait(act, p, 32)
                    pv_done.wait(act, p, 0, lag=1)
                    act.copy(v["hi", par][:, 0:TT, :], v_raw[:, 0:TT, :]).then_inc(v_hi_done.sem, 1)
                    act.copy(v["hi", par][0:META, TT, :], v_raw[0:META, TT, :]).then_inc(v_hi_done.sem, 1)

                def segment(cur, nxt, p, which):
                    for k in range(TILES):
                        n = rows(k)
                        if cur is not None:
                            h, i = cur
                            e = i * TILES + k + 1
                            p_dif.wait(act, h, e)
                            act.activation(prob[k % RING][0:n, :], prob[k % RING][0:n, :], ACT.Exp,
                                           scale=SM_SCALE).then_inc(p_exp.sem, 1)
                        if nxt is not None:
                            x, i = nxt
                            s_done.wait(act, x, i * TILES + k + 1)
                            p_dif.wait(act, x, i * TILES + k + 1, lag=1)
                            act.copy(scores[i][0:n, k, :], s_bank[(i + k) % 2][0:n, :]).then_inc(s_kept.sem, 1)
                        if cur is not None:
                            h, i = cur
                            p_exp.wait(act, h, e)
                            pv_done.wait(act, h, e - RING)
                            act.copy(prob_hi[k % RING][0:n, :], prob[k % RING][0:n, :]).then_inc(p_hi.sem, 1)
                        if k == 2 and p is not None:
                            if which == 0:
                                values(p)
                            else:
                                weights(p, 2)
                    if cur is not None:
                        h, i = cur
                        sum_done.wait(act, h, i + 1)
                        o_scaled.wait(act, h, i)
                        act.activation(inv[:], sum_bank[:], ACT.Ln).then_inc(inv_done.sem, 1)
                        inv_done.wait(act, h, 2 * i + 1)
                        act.activation(inv[:], inv[:], ACT.Exp, scale=-1.0).then_inc(inv_done.sem, 1)

                act.preload_act_table_set("natural_log_exp_and_others")

                def both(p, h):
                    (cur0, nxt0), (cur1, nxt1) = segments(p, h)
                    if p is not None:
                        for i in range(4):
                            piece(p, i)
                    if h is not None:
                        spread_keep(h, 0)
                    if p is not None:
                        piece(p, 4)
                    segment(cur0, nxt0, p, 0)
                    if p is not None:
                        piece(p, 5)
                    if h is not None:
                        spread_keep(h, 1)
                    if p is not None:
                        piece(p, 6)
                    segment(cur1, nxt1, p, 1)

                iterations(act, both)

            @block.vector
            def _(dve):
                def piece(p, i):
                    name, _, _, _, a, w, src = PIECES[i]
                    if name == "k":
                        par = p.base % 2
                        piece_hi.wait(dve, p, i + 1)
                        dve.tensor_tensor(k_nope["lo", par][:, a:a + w], src[:, 0:w],
                                          k_nope["hi", par][:, a:a + w].bitcast(F32),
                                          ALU.subtract).then_inc(piece_read.sem, 1)
                        return
                    half = int(name[-1])
                    if name.startswith("nope"):
                        piece_hi.wait(dve, p, i + 1)
                        dve.tensor_tensor(q_nope["lo", half][:], src[:], q_nope["hi", half][:].bitcast(F32),
                                          ALU.subtract).then_inc(piece_read.sem, 1)
                    else:
                        piece_done.wait(dve, p, i + 1)
                        rope_lo.wait(dve, p, half)
                        dve.tensor_tensor(q_turned[:], src[:], table[:, a:a + w],
                                          ALU.mult).then_inc(piece_read.sem, 1)

                def find_max(h, i):
                    top_turned.wait(dve, h, i + 1)
                    dve.tensor_reduce(q_max[:], max_bank[:].rearrange("p (j k) -> p j k", k=P), AX.X,
                                      ALU.max).then_inc(q_max_done.sem, 1)

                def subtract(cur, k):
                    h, i = cur
                    e, n = i * TILES + k + 1, rows(k)
                    if k == 0:
                        spread_kept.wait(dve, h, i + 1)
                    s_kept.wait(dve, h, e)
                    p_lo.wait(dve, h, e - RING)
                    before = i * 8 + k - RING
                    p_sum.wait(dve, h, before if k > RING else i * 8 + 1 if k == RING else i * 8 - RING + k + 1)
                    dve.tensor_tensor(prob[k % RING][0:n, :], scores[i][0:n, k, :], spread[0:n, :],
                                      ALU.subtract).then_inc(p_dif.sem, 1)

                def low(cur, k):
                    h, i = cur
                    e, n = i * TILES + k + 1, rows(k)
                    p_hi.wait(dve, h, e)
                    dve.tensor_tensor(prob_lo[k % RING][0:n, :], prob[k % RING][0:n, :],
                                      prob_hi[k % RING][0:n, :].bitcast(F32), ALU.subtract).then_inc(p_lo.sem, 1)

                def running(nxt, k):
                    if k == 0:
                        return
                    x, i = nxt
                    n = rows(k)
                    s_kept.wait(dve, x, i * TILES + k + 1)
                    if k == 1:
                        top_turned.wait(dve, x, i)
                        a = scores[i][0:n, 0, :]
                    else:
                        top_done.wait(dve, x, i * 8 + k - 1)
                        a = top[0:n, :]
                    dve.tensor_tensor(top[0:n, :], a, scores[i][0:n, k, :], ALU.max).then_inc(top_done.sem, 1)

                def segment(cur, nxt):
                    if cur is not None:
                        subtract(cur, 0)
                        subtract(cur, 1)
                    for k in range(TILES):
                        if nxt is not None:
                            running(nxt, k)
                        if cur is not None:
                            low(cur, k)
                            if k + 2 < TILES:
                                subtract(cur, k + 2)
                    if nxt is not None:
                        find_max(*nxt)
                    if cur is not None:
                        h, i = cur
                        inv_done.wait(dve, h, 2 * i + 2)
                        mixed_out[i].wait(dve, h, 16, lag=1)
                        dve.tensor_tensor(mixed[i][:], o_bank[i][:], inv[:], ALU.mult).then_inc(o_scaled.sem, 1)

                def both(p, h):
                    (cur0, nxt0), (cur1, nxt1) = segments(p, h)
                    if p is not None:
                        for i in range(5):
                            piece(p, i)
                    segment(cur0, nxt0)
                    if p is not None:
                        piece(p, 5)
                        piece(p, 6)
                    segment(cur1, nxt1)

                iterations(dve, both)

            @block.tensor
            def _(pe):
                def project(p, i):
                    _, first, n, lat, a, w, out = PIECES[i]
                    if i == 0:
                        w_lo_done.wait(pe, p, 1)
                    piece_read.wait(pe, p, BEFORE[i])
                    for k in range(n):
                        last = three(pe, out[:, 0:w], w_hi[:, first + k, :], w_lo[:, first + k, :],
                                     lat["hi"][:, k, a:a + w], lat["lo"][:, k, a:a + w], k == 0, k == n - 1)
                    last.then_inc(piece_done.sem, 1)

                def score(nxt, k):
                    x, i = nxt
                    par = x.base % 2
                    if k == 0:
                        piece_read.wait(pe, x, 4 + 2 * i)
                        rope_lo.wait(pe, x, i + 1)
                    s_kept.wait(pe, x, i * TILES + k - 1)
                    if k == 0:
                        s_kept.wait(pe, x, i * TILES)
                    out = s_bank[(i + k) % 2][:]
                    ks = slice(k * P, (k + 1) * P)
                    three(pe, out, k_nope["hi", par][:, ks], k_nope["lo", par][:, ks], q_nope["hi", i][:],
                          q_nope["lo", i][:], True, False)
                    three(pe, out, kr["hi"][:, ks], kr["lo"][:, ks], q_rope["hi", i][:], q_rope["lo", i][:], False,
                          True).then_inc(s_done.sem, 1)

                def multiply(cur, k):
                    h, i = cur
                    par, n = h.base % 2, rows(k)
                    if k == 0:
                        v_lo_done.wait(pe, h, 2)
                        o_scaled.wait(pe, h, i - 1)
                    p_lo.wait(pe, h, i * TILES + k + 1)
                    three(pe, o_bank[i][:], v["hi", par][0:n, k, :], v["lo", par][0:n, k, :],
                          prob_hi[k % RING][0:n, :], prob_lo[k % RING][0:n, :], k == 0,
                          k == TILES - 1).then_inc(pv_done.sem, 1)

                def turn_max(nxt):
                    x, i = nxt
                    top_done.wait(pe, x, i * 8 + 8)
                    spread_kept.wait(pe, x, i)
                    for j in range(HALF // P):
                        js = slice(j * P, (j + 1) * P)
                        last = pe.transpose(max_bank[:, js], top[:, js], t.const("ident"))
                    last.then_inc(top_turned.sem, 1)

                def spread_max(h, i):
                    q_max_done.wait(pe, h, i + 1)
                    for j in range(HALF // P):
                        last = pe.matmul(max_bank[:, j * P:(j + 1) * P], q_max[:, j:j + 1].to_broadcast([P, P]),
                                         t.const("ident"), start=True, stop=True)
                    last.then_inc(spread_done.sem, 1)

                def segment(cur, nxt):
                    SKEW = 2
                    for step in range(TILES + SKEW):
                        if nxt is not None and step < TILES:
                            score(nxt, step)
                        if cur is not None and step >= SKEW:
                            multiply(cur, step - SKEW)
                    if nxt is not None:
                        turn_max(nxt)
                    if cur is not None:
                        h, i = cur
                        p_sum.wait(pe, h, i * 8 + 8)
                        inv_done.wait(pe, h, 2 * i - 1)
                        pe.matmul(sum_bank[:], t.const("ones"), prob_sum[:], start=True, stop=True
                                  ).then_inc(sum_done.sem, 1)

                pe.wait_ge(zeroed, 4)

                def both(p, h):
                    (cur0, nxt0), (cur1, nxt1) = segments(p, h)
                    if p is not None:
                        for i in range(3):
                            project(p, i)
                    if h is not None:
                        spread_max(h, 0)
                    if p is not None:
                        project(p, 3)
                        project(p, 4)
                    segment(cur0, nxt0)
                    if p is not None:
                        project(p, 5)
                    if h is not None:
                        spread_max(h, 1)
                    if p is not None:
                        project(p, 6)
                    segment(cur1, nxt1)

                iterations(pe, both)


def output_and_ffn(nc, t, weights):
    with ExitStack() as c:
        def sb(name, shape, dt=F32):
            return c.enter_context(nc.sbuf_tensor(name, shape, dt))

        def shared(*tensors):
            with ExitStack() as place:
                return [place.enter_context(nc.sbuf_tensor(n, shape, dt)) for n, shape, dt in tensors]

        both_parts = ("hi", "lo")
        h2_last, = shared(("h2_second", [P, KT, HALF], F32))
        acts = [{x: sb(f"ffn_in{i}_{x}", [P, KT, HALF], F32R) for x in both_parts} for i in range(2)]
        w_raw, w_hi, w_lo = weights.blocks()
        square = [sb(f"f_square{i}", [P, HALF]) for i in range(2)]
        rs = sb("f_rs", [P, HALF])
        mixed_hi2, first_squares, x_res, mixed_lo2, h_first, squares, _, normed, rs2 = shared(
            ("mixed_second_hi", [P, KT, HALF], F32R), ("h_squares", [P, FT - 2 * KT, HALF], F32),
            ("x_res", [P, KT, HALF], F32), ("mixed_second_lo", [P, KT, HALF], F32R),
            ("h_first", [P, KT, HALF], F32), ("h_squares_ring", [P, 2, HALF], F32),
            ("unused", [P, FT - 2 * KT - 5, HALF], F32), ("normed", [P, 2, HALF], F32), ("f_rs2", [P, HALF], F32))
        hidden = {x: sb(f"hidden_{x}", [P, FT, HALF], F32R) for x in both_parts}
        y = sb("ffn_out", [P, KT, HALF])
        silu, prod, sq_sum = sb("silu", [P, HALF]), sb("prod", [P, HALF]), sb("square_sum", [P, HALF])
        h2 = square
        bank = [c.enter_context(nc.psum_tensor(f"f_bank{i}", [P, HALF], F32)) for i in range(8)]
        gate_bank, up_bank, y_bank, sum_bank = bank[4], bank[5], bank[6:8], bank[2]

        mixed = [acts[1], {"hi": mixed_hi2, "lo": mixed_lo2}]
        h = [h_first[:], y[:]]
        x_res, rs2 = x_res[:], rs2[:]
        mixed_raw = [y[:], x_res]
        MIXED_LOADS = [(0, 0, 2), (0, 2, 2), (0, 4, 4), (1, 0, 4), (1, 4, 4)]
        ring = [squares[:, i, :] for i in range(2)]
        h_square = {0: [first_squares[:, m, :] for m in range(FT - 2 * KT)] + ring, 1: ring}
        normed = [normed[:, i, :] for i in range(2)]
        y_sum, h_sum = silu, sq_sum
        out_sum_bank, h_sum_bank = bank[2], bank[3]

        sem = t.sem
        w_in = [sem(f"fw_in{i}") for i in range(2)]
        w_hi_done, w_lo_done = sem("fw_hi_done"), sem("fw_lo_done")
        OUT_BLOCKS = 2 * KT
        FFN_BLOCKS = 2 * FT + 3 * KT
        m_in = [sem(f"m_in{i}") for i in range(len(MIXED_LOADS))]
        x_in, m_hi, m_lo = sem("xres_in"), sem("m_hi"), sem("m_lo")
        o_done, o_copied, o_squared, o_added, o_summed, o_rs = (
            sem(f"out_{n}") for n in ("done", "copied", "squared", "added", "summed", "rs"))
        o_scaled, h_done, h_squared, h_added, h_summed, h_rs = (
            sem(n) for n in ("out_scaled", "h_done", "h_squared", "h_added", "h_summed", "h_rs"))
        n_done, n_hi, n_lo, h_out, h_zeroed = sem("n_done"), sem("n_hi"), sem("n_lo"), sem("h_out"), sem("h_zeroed")

        def signal(name, per):
            return Signal(sem(name), per)

        gate_done, up_done, sig_done, silu_done, prod_done, hid_hi, hid_lo = (
            signal(n, 1) for n in ("ffn_gate_done", "ffn_up_done", "ffn_sig_done", "ffn_silu_done",
                                   "ffn_prod_done", "hidden_hi_done", "hidden_lo_done"))
        w_used, y_copied, y_squared, y_added = (signal("down_used", 6), signal("f_copied", 2),
                                                signal("f_squared", 2), signal("f_added", 2))
        zeroed, summed, rs_done = sem("sum_zeroed"), sem("f_summed"), sem("f_rs_done")
        f_scaled, out_added, stored = sem("f_scaled"), sem("result_added"), sem("result_stored")
        h2_in = [sem(f"h2_in{i}") for i in range(2)]
        MP = KT // 2

        def tiles(eng, s, body, *stages):
            done = 0
            for kind, beside in stages:
                if kind == "one":
                    body(At(s * FT + done), beside)
                    done += 1
                    continue
                for i in range(2):
                    body(At(s * FT + done + i), lambda: beside(i, At(0)))
                with eng.Fori(0, KT // 2 - 1) as j:
                    for i in range(2):
                        body(At(s * FT + done + 2 + i, j, 2), lambda: beside(i, At(1, j)))
                done += KT
            body(At(s * FT + done), nothing)
            with eng.Fori(0, FT - done - 1) as j:
                body(At(s * FT + done + 1, j), nothing)

        def nothing():
            pass

        def pairs(eng, s, body):
            body(At(s * MP), True)
            with eng.Fori(0, MP - 2) as j:
                body(At(s * MP + 1, j), True)
            body(At(s * MP + MP - 1), s == 0)

        def up_to(per, at, s, k):
            stage = s * (FFN_BLOCKS - 2 * FT) if per == 2 else 2 * FT + s * (FFN_BLOCKS - 6 * MP)
            return at.count(per, OUT_BLOCKS + stage + k)

        def landed(per, at, s, k):
            stage = s * (FFN_BLOCKS - 2 * FT) if per == 2 else 2 * FT + s * (FFN_BLOCKS - 6 * MP)
            return at.count(8 * per, 16 * ((OUT_BLOCKS + stage + k + 1) // 2))

        h2_last_in = sem("h2_last_in")
        BY_POOL = [1, 3, 5]
        last_added = {x: sem(f"result_added_by_{x}") for x in ("dve", "pool")}

        def add_last(eng, by, m):
            eng.wait_ge(f_scaled, KT + m + 1)
            eng.wait_ge(h2_last_in, 16)
            eng.tensor_tensor(y[:, m, :], y[:, m, :], h2_last[:, m, :], ALU.add).then_inc(last_added[by], 1)

        with nc.Block() as block:
            @block.sync
            def _(sp):
                HALF_PAIRS = FFN_BLOCKS // 2

                def load(s, j):
                    for i in range(2):
                        before = OUT_BLOCKS + s * FFN_BLOCKS + i - 2
                        sp.wait_ge(w_hi_done, 2 * j + before)
                        sp.wait_ge(w_lo_done, 2 * j + before)
                        sp.dma_start(w_raw[i][:], dram_block(t.d["w_ffn"], 2 * j + i)).then_inc(w_in[i], 16)

                def load_h2(i, pair):
                    if pair.j is None and pair.base == 0:
                        sp.wait_ge(summed, 1)
                    else:
                        sp.wait_ge(out_added, pair.count(2, i + 1, lag=1))
                    src = t.d_h2[:, bass.ds(pair.index() * 2 + i, 1), 0:HALF]
                    sp.dma_start(h2[i][:].unsqueeze(1), src).then_inc(h2_in[i], 16)

                def store(s, m, n):
                    if s:
                        sp.wait_ge(last_added["dve"], sum(k not in BY_POOL for k in range(m + n)))
                        sp.wait_ge(last_added["pool"], sum(k in BY_POOL for k in range(m + n)))
                    else:
                        sp.wait_ge(out_added, m + n)
                    sp.dma_start(t.out[:, m:m + n, s * HALF:(s + 1) * HALF], y[:, m:m + n, :]).then_inc(stored, 16)

                def load_out(b):
                    if b > 2:
                        sp.wait_ge(w_hi_done, b - 2)
                        sp.wait_ge(w_lo_done, b - 2)
                    sp.dma_start(w_raw[b % 2][:], t.d["w_out"][b % KT]).then_inc(w_in[b % 2], 16)

                def store_h(s):
                    sp.wait_ge(h_done, KT * (s + 1))
                    sp.dma_start(t.d_h2[:, :, s * HALF:(s + 1) * HALF], h[s]).then_inc(h_out, 16)

                for i, (half, first, n) in enumerate(MIXED_LOADS):
                    src = t.d_mixed[first:first + n, :, half * HALF:(half + 1) * HALF].rearrange("k p n -> p k n")
                    sp.dma_start(mixed_raw[half][:, first:first + n, :], src).then_inc(m_in[i], 16)
                    if i < 2:
                        load_out(i + 1)
                sp.wait_ge(m_hi, 2 * KT)
                sp.wait_ge(m_lo, 2 * KT)
                sp.dma_start(x_res, t.d["x"][:, :, 0:HALF]).then_inc(x_in, 16)
                for b in range(3, OUT_BLOCKS):
                    if b == OUT_BLOCKS - 2:
                        store_h(0)
                        sp.dma_start(x_res, t.d["x"][:, :, HALF:SEQ]).then_inc(x_in, 16)
                    load_out(b)
                BEFORE_STORE = KT + 4
                with sp.Fori(0, BEFORE_STORE) as j:
                    load(0, j)
                store_h(1)
                with sp.Fori(0, HALF_PAIRS - BEFORE_STORE) as j:
                    load(0, j + BEFORE_STORE)
                load(1, 0)
                load(1, 1)
                load(1, 2)
                sp.wait_ge(h_out, 32)
                for i in range(2):
                    load_h2(i, At(0))
                    load(1, i + 3)
                with sp.Fori(0, KT // 2 - 1) as j:
                    for i in range(2):
                        load_h2(i, At(1, j))
                        load(1, j * 2 + (i + 5))
                store(0, 0, KT)
                with sp.Fori(0, HALF_PAIRS - KT - 3) as j:
                    load(1, j + (KT + 3))
                sp.wait_ge(up_done.sem, 2 * FT)
                sp.dma_start(h2_last[:], t.d_h2[:, :, HALF:SEQ]).then_inc(h2_last_in, 16)
                for m in range(0, KT, 2):
                    store(1, m, 2)
                sp.wait_ge(stored, 16 * 5)

            @block.gpsimd
            def _(pool):
                def add_square(e):
                    m = e % KT
                    if m == 0:
                        return
                    pool.wait_ge(o_squared, e + 1)
                    if m == 1 and e > KT:
                        pool.wait_ge(o_summed, 1)
                    if m > 1:
                        pool.wait_ge(o_added, e // KT * (KT - 1) + m - 1)
                    pool.tensor_tensor(y_sum[:], (square[(e - 1) % 2] if m == 1 else y_sum)[:], square[e % 2][:],
                                       ALU.add).then_inc(o_added, 1)

                for b in range(1, OUT_BLOCKS):
                    pool.wait_ge(w_hi_done, b)
                    pool.tensor_tensor(w_lo[b % 2][:], w_raw[b % 2][:], w_hi[b % 2][:].bitcast(F32),
                                       ALU.subtract).then_inc(w_lo_done, 1)
                    add_square(b - 1)
                add_square(OUT_BLOCKS - 1)
                with pool.Fori(0, FFN_BLOCKS) as j:
                    for i in range(2):
                        pool.wait_ge(w_hi_done, 2 * j + (OUT_BLOCKS + i))
                        pool.tensor_tensor(w_lo[i][:], w_raw[i][:], w_hi[i][:].bitcast(F32),
                                           ALU.subtract).then_inc(w_lo_done, 1)
                for m in BY_POOL:
                    add_last(pool, "pool", m)

            @block.scalar
            def _(act):
                def weight_hi(per, at, s, k):
                    act.wait_ge(w_in[k % 2], landed(per, at, s, k))
                    act.copy(w_hi[k % 2][:], w_raw[k % 2][:]).then_inc(w_hi_done, 1)

                def feed(s):
                    def tile(at, beside):
                        up_done.wait(act, at, 1, lag=1)
                        weight_hi(2, at, s, 1)
                        gate_done.wait(act, at, 1)
                        prod_done.wait(act, at, 1, lag=1)
                        act.activation(silu[:], gate_bank[:], ACT.Sigmoid).then_inc(sig_done.sem, 1)
                        weight_hi(2, at, s, 2)
                        beside()
                        prod_done.wait(act, at, 1)
                        act.copy(hidden["hi"][:, bass.ds(at.index() - s * FT, 1), :],
                                 prod[:].unsqueeze(1)).then_inc(hid_hi.sem, 1)
                    return tile

                def down(s):
                    def pair(at, more):
                        if at.j is None and at.base == s * MP:
                            act.wait_ge(up_done.sem, (s + 1) * FT)
                        for x in range(6):
                            if x < 5 or more:
                                w_used.wait(act, at, x)
                                weight_hi(6, at, s, x + 1)
                            if x % 3 < 2:
                                continue
                            i = x // 3
                            w_used.wait(act, at, 3 * i + 3)
                            m = bass.ds(at.index() * 2 + (i - s * KT), 1)
                            act.copy(y[:, m, :], y_bank[i][:].unsqueeze(1)).then_inc(y_copied.sem, 1)
                            y_added.wait(act, at, i + 1, lag=1)
                            act.activation(square[i][:], y_bank[i][:], ACT.Square).then_inc(y_squared.sem, 1)
                    return pair

                def inverse_rms(s):
                    act.wait_ge(summed, s + 1)
                    if s:
                        act.wait_ge(f_scaled, s * KT)
                    else:
                        act.wait_ge(o_scaled, 2 * KT)
                    act.activation(rs[:], sum_bank[:], ACT.Ln, bias=t.gain("eps", 0), scale=1.0 / D
                                   ).then_inc(rs_done, 1)
                    act.wait_ge(rs_done, 2 * s + 1)
                    act.activation(rs[:], rs[:], ACT.Exp, scale=-0.5).then_inc(rs_done, 1)

                def weight_hi_out(b):
                    act.wait_ge(w_in[b % 2], 16 * ((b + 1) // 2))
                    if b >= 2:
                        act.wait_ge(o_done, b - 1)
                    act.copy(w_hi[b % 2][:], w_raw[b % 2][:]).then_inc(w_hi_done, 1)

                def inverse_rms_of(dst, src, summed_, used, done, s):
                    act.wait_ge(summed_, s + 1)
                    if s:
                        act.wait_ge(used, KT)
                    act.activation(dst, src[:], ACT.Ln, bias=t.gain("eps", 0), scale=1.0 / D).then_inc(done, 1)
                    act.wait_ge(done, 2 * s + 1)
                    act.activation(dst, dst, ACT.Exp, scale=-0.5).then_inc(done, 1)

                def o_inverse_rms(s):
                    inverse_rms_of(rs[:], out_sum_bank, o_summed, o_scaled, o_rs, s)

                def h_inverse_rms(s):
                    inverse_rms_of(rs2, h_sum_bank, h_summed, n_done, h_rs, s)

                def mixed_hi(q):
                    half, k = q // KT, q % KT
                    for i, (of_half, first, n) in enumerate(MIXED_LOADS):
                        if of_half == half and first <= k < first + n:
                            act.wait_ge(m_in[i], 16)
                    act.copy(mixed[half]["hi"][:, k, :], mixed_raw[half][:, k, :]).then_inc(m_hi, 1)

                def projected(b):
                    s, m = b // KT, b % KT
                    act.wait_ge(o_done, b + 1)
                    act.copy(h[s][:, m, :], bank[b % 2][:]).then_inc(o_copied, 1)
                    if b >= 2:
                        before = b - 2
                        act.wait_ge(o_added, before // KT * (KT - 1) + max(before % KT, 1))
                    act.activation(square[b % 2][:], bank[b % 2][:], ACT.Square).then_inc(o_squared, 1)

                def square_h(m):
                    act.wait_ge(h_done, m + 1)
                    act.activation(h_square[0][m], h[0][:, m, :], ACT.Square).then_inc(h_squared, 1)

                def normed_hi(m):
                    act.wait_ge(n_done, m + 1)
                    act.copy(acts[0]["hi"][:, m, :], normed[m % 2]).then_inc(n_hi, 1)

                def square_h_step(i, pair):
                    act.wait_ge(h_done, pair.count(2, KT + i + 1))
                    act.wait_ge(h_added, pair.count(2, KT + i - 1))
                    src = h[1][:, bass.ds(pair.index() * 2 + i, 1), :]
                    act.activation(h_square[1][i].unsqueeze(1), src, ACT.Square).then_inc(h_squared, 1)

                def normed_hi_step(i, pair):
                    act.wait_ge(n_done, pair.count(2, KT + i + 1))
                    act.copy(acts[1]["hi"][:, bass.ds(pair.index() * 2 + i, 1), :], normed[i].unsqueeze(1)
                             ).then_inc(n_hi, 1)

                act.preload_act_table_set("natural_log_exp_and_others")
                for q in range(3):
                    mixed_hi(q)
                weight_hi_out(1)
                for q in range(3, 2 * KT):
                    mixed_hi(q)
                beside = {0: [lambda m=m: square_h(m) for m in (0, 1)],
                          1: [lambda m=m: square_h(m) for m in (2, 3, 4, 5)],
                          2: [lambda m=m: square_h(m) for m in (6, 7)], 3: [lambda: h_inverse_rms(0)],
                          4: [lambda m=m: normed_hi(m) for m in (0, 1, 2)],
                          5: [lambda m=m: normed_hi(m) for m in (3, 4, 5)],
                          6: [lambda m=m: normed_hi(m) for m in (6, 7)]}
                for b in range(OUT_BLOCKS):
                    if 2 <= b + 1 < OUT_BLOCKS:
                        weight_hi_out(b + 1)
                    elif b + 1 == OUT_BLOCKS:
                        act.wait_ge(o_done, b)
                        weight_hi(2, At(0), 0, 0)
                    if b == KT:
                        o_inverse_rms(0)
                    projected(b)
                    if b >= KT:
                        for step in beside.get(b - KT, []):
                            step()
                act.wait_ge(h_out, 16)
                act.wait_ge(o_done, OUT_BLOCKS)
                tiles(act, 0, feed(0), ("one", lambda: o_inverse_rms(1)), ("over", square_h_step), ("one", nothing),
                      ("one", lambda: h_inverse_rms(1)), ("over", normed_hi_step))
                act.wait_ge(h_out, 32)
                pairs(act, 0, down(0))
                tiles(act, 1, feed(1), ("one", nothing), ("one", lambda: inverse_rms(0)))
                act.wait_ge(out_added, KT)
                act.wait_ge(stored, 16)
                pairs(act, 1, down(1))
                inverse_rms(1)

            @block.vector
            def _(dve):
                def feed(s):
                    def tile(at, beside):
                        sig_done.wait(dve, at, 1)
                        dve.tensor_tensor(silu[:], silu[:], gate_bank[:], ALU.mult).then_inc(silu_done.sem, 1)
                        beside()
                        up_done.wait(dve, at, 1)
                        silu_done.wait(dve, at, 1)
                        hid_hi.wait(dve, at, 1, lag=1)
                        hid_lo.wait(dve, at, 1, lag=1)
                        dve.tensor_tensor(prod[:], silu[:], up_bank[:], ALU.mult).then_inc(prod_done.sem, 1)
                        hid_hi.wait(dve, at, 1)
                        f = bass.ds(at.index() - s * FT, 1)
                        dve.tensor_tensor(hidden["lo"][:, f, :], prod[:].unsqueeze(1),
                                          hidden["hi"][:, f, :].bitcast(F32), ALU.subtract
                                          ).then_inc(hid_lo.sem, 1)
                    return tile

                def pair(at, more):
                    for i in range(2):
                        y_squared.wait(dve, at, i + 1)
                        y_added.wait(dve, at, i)
                        dve.tensor_tensor(sq_sum[:], sq_sum[:], square[i][:], ALU.add).then_inc(y_added.sem, 1)

                def finish(i, pair):
                    if pair.j is None and pair.base == 0:
                        dve.wait_ge(rs_done, 2)
                    m = bass.ds(pair.index() * 2 + i, 1)
                    gain = t.gains[:, bass.ds(pair.index() * 2 + (GAINS["ffn_post"] + i), 1)]
                    dve.scalar_tensor_tensor(out=y[:, m, :], in0=y[:, m, :], scalar=gain, in1=rs[:].unsqueeze(1),
                                             op0=ALU.mult, op1=ALU.mult).then_inc(f_scaled, 1)
                    dve.wait_ge(f_scaled, pair.count(2, i + 1))
                    dve.wait_ge(h2_in[i], pair.count(16, 16))
                    dve.tensor_tensor(y[:, m, :], y[:, m, :], h2[i][:].unsqueeze(1), ALU.add
                                      ).then_inc(out_added, 1)

                def mixed_lo(q):
                    dve.wait_ge(m_hi, q + 1)
                    dve.tensor_tensor(mixed[q // KT]["lo"][:, q % KT, :], mixed_raw[q // KT][:, q % KT, :],
                                      mixed[q // KT]["hi"][:, q % KT, :].bitcast(F32), ALU.subtract
                                      ).then_inc(m_lo, 1)

                def residual(s, m, gain, e):
                    dve.scalar_tensor_tensor(out=h[s][:, m, :], in0=h[s][:, m, :], scalar=gain,
                                             in1=rs[:].unsqueeze(1), op0=ALU.mult, op1=ALU.mult
                                             ).then_inc(o_scaled, 1)
                    dve.wait_ge(o_scaled, e)
                    dve.tensor_tensor(h[s][:, m, :], h[s][:, m, :], x_res[:, m, :], ALU.add).then_inc(h_done, 1)

                def add_square(src):
                    dve.tensor_tensor(h_sum[:], h_sum[:], src, ALU.add).then_inc(h_added, 1)

                def normalize(s, i, m, gain):
                    dve.scalar_tensor_tensor(out=normed[i].unsqueeze(1), in0=h[s][:, m, :], scalar=gain,
                                             in1=rs2.unsqueeze(1), op0=ALU.mult, op1=ALU.mult).then_inc(n_done, 1)

                def normed_lo(s, i, m):
                    dve.tensor_tensor(acts[s]["lo"][:, m, :], normed[i].unsqueeze(1),
                                      acts[s]["hi"][:, m, :].bitcast(F32), ALU.subtract).then_inc(n_lo, 1)

                def residual_step(i, pair):
                    if pair.j is None and pair.base == 0 and i == 0:
                        dve.wait_ge(o_rs, 4)
                        dve.wait_ge(x_in, 32)
                    residual(1, bass.ds(pair.index() * 2 + i, 1),
                             t.gains[:, bass.ds(pair.index() * 2 + (GAINS["mix_post"] + i), 1)],
                             pair.count(2, KT + i + 1))
                    if pair.j is not None or pair.base or i:
                        dve.wait_ge(h_squared, pair.count(2, KT + i))
                        dve.wait_ge(h_added, pair.count(2, KT + i - 1))
                        add_square(h_square[1][1 - i])

                def last_square():
                    dve.wait_ge(h_squared, 2 * KT)
                    dve.wait_ge(h_added, 2 * KT - 1)
                    add_square(h_square[1][1])

                def normalize_step(i, pair):
                    if pair.j is None and pair.base == 0 and i == 0:
                        dve.wait_ge(h_rs, 4)
                    m = bass.ds(pair.index() * 2 + i, 1)
                    dve.wait_ge(n_lo, pair.count(2, KT + i - 1))
                    normalize(1, i, m, t.gains[:, bass.ds(pair.index() * 2 + (GAINS["ffn_pre"] + i), 1)])
                    dve.wait_ge(n_hi, pair.count(2, KT + i + 1))
                    normed_lo(1, i, m)

                def clear_h_sum(s):
                    if s:
                        dve.wait_ge(h_summed, s)
                    dve.memset(h_sum[:], 0.0).then_inc(h_zeroed, 1)
                    dve.wait_ge(h_zeroed, s + 1)

                for q in range(2 * KT):
                    mixed_lo(q)
                clear_h_sum(0)
                dve.wait_ge(o_rs, 2)
                dve.wait_ge(x_in, 16)
                for m in range(KT):
                    residual(0, slice(m, m + 1), t.gain("mix_post", m), m + 1)
                for m in range(KT):
                    dve.wait_ge(h_squared, m + 1)
                    if m:
                        dve.wait_ge(h_added, m)
                    add_square(h_square[0][m])
                dve.wait_ge(h_rs, 2)
                for m in range(KT + 1):
                    if m < KT:
                        if m >= 2:
                            dve.wait_ge(n_lo, m - 1)
                        normalize(0, m % 2, slice(m, m + 1), t.gain("ffn_pre", m))
                    if m:
                        dve.wait_ge(n_hi, m)
                        normed_lo(0, (m - 1) % 2, slice(m - 1, m))
                clear_h_sum(1)
                dve.wait_ge(h_out, 16)
                tiles(dve, 0, feed(0), ("one", nothing), ("over", residual_step), ("one", last_square),
                      ("one", nothing), ("over", normalize_step))
                dve.wait_ge(h_summed, 2)
                dve.memset(sq_sum[:], 0.0).then_inc(zeroed, 1)
                dve.wait_ge(zeroed, 1)
                pairs(dve, 0, pair)

                def clear_sum():
                    dve.wait_ge(summed, 1)
                    dve.memset(sq_sum[:], 0.0).then_inc(zeroed, 1)

                tiles(dve, 1, feed(1), ("one", nothing), ("one", clear_sum), ("over", finish))
                dve.wait_ge(zeroed, 2)
                pairs(dve, 1, pair)
                dve.wait_ge(rs_done, 4)
                for m in range(KT + 1):
                    if m < KT:
                        dve.scalar_tensor_tensor(out=y[:, m, :], in0=y[:, m, :], scalar=t.gain("ffn_post", m),
                                                 in1=rs[:], op0=ALU.mult, op1=ALU.mult).then_inc(f_scaled, 1)
                    if m and m - 1 not in BY_POOL:
                        add_last(dve, "dve", m - 1)

            @block.tensor
            def _(pe):
                def multiply(out, slot, x, tile, first, last):
                    n = len(tile)
                    for k in range(n):
                        ins = three(pe, out[:], w_hi[slot][:, k, :], w_lo[slot][:, k, :], x["hi"][:, tile[k], :],
                                    x["lo"][:, tile[k], :], first and k == 0, last and k == n - 1)
                    return ins

                def feed(s):
                    def tile(at, beside):
                        pe.wait_ge(w_lo_done, up_to(2, at, s, 0))
                        silu_done.wait(pe, at, 1, lag=1)
                        multiply(gate_bank, 0, acts[s], range(KT), True, True).then_inc(gate_done.sem, 1)
                        pe.wait_ge(w_lo_done, up_to(2, at, s, 1))
                        prod_done.wait(pe, at, 1, lag=1)
                        multiply(up_bank, 1, acts[s], range(KT), True, True).then_inc(up_done.sem, 1)
                        beside()
                    return tile

                def down(s):
                    def pair(at, more):
                        for x in range(6):
                            i, part = x // 3, x % 3
                            pe.wait_ge(w_lo_done, up_to(6, at, s, x))
                            if part == 0:
                                y_squared.wait(pe, at, i + 1, lag=1)
                            if x == 0:
                                pe.wait_ge(hid_lo.sem, (s + 1) * FT)
                            ks = range(part * KT, min((part + 1) * KT, FT))
                            ins = multiply(y_bank[i], x % 2, hidden, ks, part == 0, part == 2)
                            ins.then_inc(w_used.sem, 1)
                    return pair

                def add_up(s):
                    y_added.wait(pe, At(s * MP + MP - 1), 2)
                    if s:
                        pe.wait_ge(rs_done, 2)
                    else:
                        pe.wait_ge(o_rs, 4)
                    pe.matmul(sum_bank[:], t.const("ones"), sq_sum[:], start=True, stop=True).then_inc(summed, 1)

                def project(b, between=(None, None)):
                    s = b // KT
                    if b:
                        pe.wait_ge(w_lo_done, b)
                    if b >= 2:
                        pe.wait_ge(o_squared, b - 1)
                    for k in range(KT):
                        if b % KT == 0:
                            pe.wait_ge(m_lo, s * KT + k + 1)
                        last = three(pe, bank[b % 2][:], w_hi[b % 2][:, k, :], w_lo[b % 2][:, k, :],
                                     mixed[s]["hi"][:, k, :], mixed[s]["lo"][:, k, :], k == 0, k == KT - 1)
                        if k == between[0]:
                            between[1]()
                    last.then_inc(o_done, 1)

                def add_up_o(s):
                    pe.wait_ge(o_added, (KT - 1) * (s + 1))
                    if s:
                        pe.wait_ge(o_rs, 2)
                    pe.matmul(out_sum_bank[:], t.const("ones"), y_sum[:], start=True, stop=True).then_inc(o_summed, 1)

                def add_up_h(s):
                    pe.wait_ge(h_added, KT * (s + 1))
                    if s:
                        pe.wait_ge(h_rs, 2)
                    pe.matmul(h_sum_bank[:], t.const("ones"), h_sum[:], start=True, stop=True).then_inc(h_summed, 1)

                for m in range(KT):
                    project(m)
                for m in range(KT):
                    project(KT + m, {0: (4, lambda: add_up_o(0)), 4: (0, lambda: add_up_h(0))}.get(m, (None, None)))
                pe.wait_ge(n_lo, KT)
                add_up_o(1)
                tiles(pe, 0, feed(0), *[("one", nothing)] * (KT + 1), ("one", lambda: add_up_h(1)))
                pairs(pe, 0, down(0))
                pe.wait_ge(n_lo, 2 * KT)
                tiles(pe, 1, feed(1), ("one", lambda: add_up(0)))
                pairs(pe, 1, down(1))
                add_up(1)


class Shared:

    def __init__(self, nc, ctx):
        self.nc, self.sems, self.taken = nc, ctx, []

    def sem(self, name):
        handle = self.sems.enter_context(self.nc.semaphore(name))
        self.taken.append(handle)
        return handle

    def gain(self, name, k):
        a = GAINS[name] + k
        return self.gains[:, a:a + 1]

    def const(self, name):
        i = [n for n, _ in CONSTS].index(name)
        return self.consts[:, i * P:(i + 1) * P]


GAIN_WIDTHS = [("mix_pre", KT), ("cq", QT), ("ckv", KVT), ("hgrn", 1), ("mix_post", KT), ("ffn_pre", KT),
               ("ffn_post", KT), ("eps", 1)]
GAINS, _at = {}, 0
for _name, _n in GAIN_WIDTHS:
    GAINS[_name] = _at
    _at += _n
N_GAINS = _at


CONSTS = [("ones", P), ("ident", P), ("fold", P), ("mask_f_near", P), ("mask_f_far", P), ("mask_b_near", P),
          ("mask_b_far", P)]
N_CONSTS = P * len(CONSTS)


def constants():
    s, q = np.arange(P)[:, None], np.arange(P)[None, :]
    ss, qq = s // SUB, q // SUB
    parts = [np.ones((P, P)), s == q, s % 64 == q % 64, (ss == qq) & (s <= q), ss < qq, (ss == qq) & (s > q),
             ss > qq]
    return np.ascontiguousarray(np.concatenate([np.asarray(x, np.float32) for x in parts], axis=1))


def rope_table():
    inv = np.float32(10000.0) ** (-np.arange(0, ROPE, 2, dtype=np.float32) / np.float32(ROPE))
    where = np.concatenate([np.arange(META, L), np.arange(META)]).astype(np.float32)
    ang = inv[:, None].astype(np.float32) * where[None, :]
    cos, sin = np.cos(ang), np.sin(ang)
    return np.ascontiguousarray(np.concatenate([cos, cos, -sin, sin], axis=0).astype(np.float32))


def bass_hybrid_encoder_layer(nc, d, out):
    with ExitStack() as ctx:
        early = ExitStack()
        t = Shared(nc, early)
        t.d = d
        t.d_v = nc.dram_tensor("values", (P, TT + 1, D), F32, kind="Internal").ap()
        t.d_mv = nc.dram_tensor("attention_values", (P, TT + 1, D), F32, kind="Internal").ap()
        t.d_mixed = nc.dram_tensor("mixed", (HEADS, P, SEQ), F32, kind="Internal").ap()
        t.d_h2 = nc.dram_tensor("h2", (P, KT, SEQ), F32, kind="Internal").ap()
        t.out = out
        t.d_ga = nc.dram_tensor("gate_out", (HEADS, P, SEQ), F32, kind="Internal").ap()
        t.d_r = nc.dram_tensor("hgrn_out", (HEADS, P, SEQ), F32, kind="Internal").ap()
        t.consts = ctx.enter_context(nc.sbuf_tensor("consts", [P, N_CONSTS], F32))
        t.gains = ctx.enter_context(nc.sbuf_tensor("gains", [P, N_GAINS], F32))
        t.lb = ctx.enter_context(nc.sbuf_tensor("lb", [P, 2 * HEADS], F32))
        t.omlb = ctx.enter_context(nc.sbuf_tensor("one_minus_lb", [P, 2 * HEADS], F32))
        t.momlb = ctx.enter_context(nc.sbuf_tensor("minus_one_minus_lb", [P, 2 * HEADS], F32))
        weights = Weights(t, lambda name, shape, dt: ctx.enter_context(nc.sbuf_tensor(name, shape, dt)))
        with nc.sbuf_tensor("raw", [P, 6 * L], F32) as raw:
            t.raw = raw
            with nc.sbuf_tensor("hn_hi", [P, KT, L], F32R) as hn_hi, nc.sbuf_tensor("hn_lo", [P, KT, L], F32R) as hn_lo:
                normalize_and_values(nc, t, hn_hi, hn_lo, weights)
                hgrn_heads(nc, t, hn_hi, hn_lo, weights)
            with ExitStack() as of_attention:
                lat = Latents(t, weights, of_attention, ctx)
                latents(nc, t, lat)
                used, t.sems = list(t.taken), ctx
                attention_heads(nc, t, weights, lat, used)
        early.close()
        output_and_ffn(nc, t, weights)


def columns(v, n):
    return np.asarray(v).reshape(n, P).T


def moving_last(w, n, m):
    return np.asarray(w).reshape(n, P, m).transpose(1, 0, 2)


def lay_out(x, meta_tokens, g_mix_pre, w_in, g_cq, g_ckv, w_uq, w_ukv, lb_logits, g_hgrn, w_o, g_mix_post,
            g_ffn_pre, w_gate, w_up, w_down, g_ffn_post):
    a = {}
    h = np.concatenate([x[0], meta_tokens], axis=0)
    a["x"] = moving_last(h.T, KT, L)
    w = np.asarray(w_in[0])
    at = np.cumsum([0, Q_RANK, KV_RANK, ROPE] + [D] * 7)
    col = dict(zip(["cq", "ckv", "kr", "q", "ff", "fb", "hi", "hg", "ga", "gh"], at))
    block = lambda name, i: moving_last(w[:, col[name] + i * P:col[name] + (i + 1) * P], KT, P)
    a["vw"] = np.stack([moving_last(w[:, col["hi"] + i * QUARTER:col["hi"] + (i + 1) * QUARTER], KT, QUARTER)
                        for i in range(4)])
    swap = np.concatenate([np.arange(ROPE), np.arange(ROPE // 2, ROPE), np.arange(ROPE // 2)])
    kr = moving_last(w[:, col["kr"] + swap], KT, P)
    a["w_hgrn"] = np.stack([block(n, h) for h in range(HEADS) for n in IN_HGRN]
                           + [kr if n == "kr" else block(n, i) for n, i in LATENTS])
    uq, ukv = np.asarray(w_uq[0]), np.asarray(w_ukv[0])
    a["w_head"] = np.stack([np.concatenate([
        moving_last(uq[:, h * (P + ROPE):h * (P + ROPE) + P], QT, P),
        moving_last(uq[:, h * (P + ROPE) + P + swap], QT, P),
        moving_last(ukv[:, h * 2 * P:h * 2 * P + P], KVT, P)], axis=1) for h in range(HEADS)]
        + [moving_last(np.asarray(w_o[0])[:, 0:P], KT, P)])
    w_v = np.concatenate([moving_last(ukv[:, h * 2 * P + P:h * 2 * P + 2 * P], KVT, P)
                               for h in range(HEADS)], axis=2)
    a["w_v"] = w_v.reshape(P, KVT, 2, HALF).transpose(2, 0, 1, 3)
    tiles = lambda m, n, k: np.stack([moving_last(np.asarray(m)[:, i * P:(i + 1) * P], k, P) for i in range(n)])
    a["w_out"] = tiles(w_o[0], KT, KT)
    gate_up = np.stack([tiles(w_gate[0], FT, KT), tiles(w_up[0], FT, KT)], axis=1).reshape(2 * FT, P, KT, P)
    down = tiles(w_down[0], KT, FT)
    down = np.concatenate([down, np.zeros((KT, P, 3 * KT - FT, P), down.dtype)], axis=2)
    down = down.reshape(KT, P, 3, KT, P).transpose(0, 2, 1, 3, 4).reshape(3 * KT, P, KT, P)
    a["w_ffn"] = np.concatenate([gate_up, down])
    a["logits"] = np.asarray(lb_logits).reshape(2, 2, HEADS, P).transpose(3, 0, 1, 2).reshape(P, 2, 2 * HEADS)
    a["gains"] = np.concatenate([
        columns(g_mix_pre[0], KT), columns(g_cq[0], QT), columns(g_ckv[0], KVT), columns(g_hgrn[0], 1),
        columns(g_mix_post[0], KT), columns(g_ffn_pre[0], KT), columns(g_ffn_post[0], KT),
        np.full((P, 1), EPS, np.float32)], axis=1)
    a["consts"], a["rope"] = constants(), rope_table()
    return {k: np.ascontiguousarray(v) for k, v in a.items()}


def kernel(**inputs):
    import concourse.bacc as bacc
    from concourse.bass_utils import run_bass_kernel_spmd

    nc = bacc.Bacc("TRN2", target_bir_lowering=False, num_devices=1)
    arrays = {f"in_{k}": v for k, v in lay_out(**inputs).items()}
    d = {k[3:]: nc.dram_tensor(k, v.shape, mybir.dt.from_np(v.dtype), kind="ExternalInput").ap()
         for k, v in arrays.items()}
    out = nc.dram_tensor("out", (P, KT, SEQ), F32, kind="ExternalOutput").ap()
    bass_hybrid_encoder_layer(nc, d, out)
    r = run_bass_kernel_spmd(nc, [arrays], core_ids=[0])
    return np.ascontiguousarray(r.results[0]["out"].transpose(2, 1, 0).reshape(SEQ, D))[None]
```
